# Optimizing a Trainium2 kernel written in Bass

```python
import math
import jax, jax.numpy as jnp
from jax import lax
import numpy as np

D_MODEL = 1024
BATCH = 1
SEQ = 256
DEPTH = 2

CHUNK = 64
N_META = 16
BLOCK_Q = 128
MIX_WIDTH = D_MODEL
A_HEADS = 8
A_HEAD_DIM = (MIX_WIDTH // 2) // A_HEADS
A_WIDTH = A_HEADS * A_HEAD_DIM
B_GROUPS = 8
B_WIDTH = MIX_WIDTH // 2
B_CONV = 3
AB_IN = 3 * A_WIDTH + 3 * B_WIDTH
CF_INNER = D_MODEL
CF_CONV = 31
PEER_HEADS = 8
PEER_KEY_DIM = 256
PEER_HALF = PEER_KEY_DIM // 2
N_KEYS = 128
N_EXPERTS = N_KEYS * N_KEYS
PEER_TOPK = 16
PEER_BLOCK = 128
N_EVEN = (DEPTH + 1) // 2
N_ODD = DEPTH // 2
EPS = 1e-6

kernel_name = "hybrid_stickbreak_shortconv_conformer_peer"

def rmsnorm(x, g):
    xf = x.astype(jnp.float32)
    y = xf * lax.rsqrt(jnp.mean(xf * xf, axis=-1, keepdims=True) + EPS) * g.astype(jnp.float32)
    return y.astype(x.dtype)

def layernorm(x, g, b):
    xf = x.astype(jnp.float32)
    mu = jnp.mean(xf, axis=-1, keepdims=True)
    var = jnp.mean(jnp.square(xf - mu), axis=-1, keepdims=True)
    y = (xf - mu) * lax.rsqrt(var + EPS) * g.astype(jnp.float32) + b.astype(jnp.float32)
    return y.astype(x.dtype)

def causal_depthwise_conv(x, w):
    K, C = w.shape
    return lax.conv_general_dilated(
        x, w[:, None, :].astype(x.dtype), window_strides=(1,), padding=[(K - 1, 0)],
        dimension_numbers=('NWC', 'WIO', 'NWC'), feature_group_count=C)

def stick_breaking_attention(q, k, v):
    B, H, L, dh = q.shape
    nb = L // BLOCK_Q
    qb = q.reshape(B, H, nb, BLOCK_Q, dh).transpose(2, 0, 1, 3, 4)
    key_pos = jnp.arange(L)
    scale = 1.0 / math.sqrt(dh)

    def block(args):
        q_blk, start = args
        z = jnp.einsum('bhqd,bhkd->bhqk', q_blk, k).astype(jnp.float32) * scale
        q_pos = start + jnp.arange(BLOCK_Q)
        mask = key_pos[None, :] < q_pos[:, None]
        log_beta = jax.nn.log_sigmoid(z)
        log_not = jnp.where(mask, jax.nn.log_sigmoid(-z), 0.0)
        log_w = log_beta + lax.cumsum(log_not, axis=3, reverse=True) - log_not
        w = jnp.where(mask, jnp.exp(log_w), 0.0)
        return jnp.einsum('bhqk,bhkd->bhqd', w.astype(v.dtype), v)

    out = lax.map(block, (qb, jnp.arange(nb, dtype=jnp.int32) * BLOCK_Q))
    return out.transpose(1, 2, 0, 3, 4).reshape(B, H, L, dh)

def mixer_ab(y, w_in, conv_w, w_out):
    B, L, _ = y.shape
    proj = y @ w_in
    q, k, v, gate_b, gate_c, h = jnp.split(proj, 6, axis=-1)
    to_heads = lambda t: t.reshape(B, L, A_HEADS, A_HEAD_DIM).transpose(0, 2, 1, 3)
    a_out = stick_breaking_attention(to_heads(q), to_heads(k), to_heads(v))
    a_out = a_out.transpose(0, 2, 1, 3).reshape(B, L, A_WIDTH)
    b_out = gate_b * causal_depthwise_conv(gate_c * h, conv_w)
    return jnp.concatenate([a_out, b_out], axis=-1) @ w_out

def mixer_conformer(y, w_pw1, b_pw1, conv_w, conv_b, ln_g, ln_b, w_pw2, b_pw2):
    z = y @ w_pw1 + b_pw1
    a, g = jnp.split(z, 2, axis=-1)
    z = a * jax.nn.sigmoid(g)
    z = causal_depthwise_conv(z, conv_w) + conv_b
    z = jax.nn.silu(layernorm(z, ln_g, ln_b))
    return z @ w_pw2 + b_pw2

def peer(y, w_q, sub_keys, u, v):
    B, L, D = y.shape
    T = B * L
    yt = y.reshape(T, D)
    q = (yt @ w_q).reshape(T, PEER_HEADS, 2, PEER_HALF)
    s = jnp.einsum('thpc,pnc->thpn', q, sub_keys).astype(jnp.float32)
    val, idx = lax.top_k(s, PEER_TOPK)
    cand = val[:, :, 0, :, None] + val[:, :, 1, None, :]
    cand_idx = idx[:, :, 0, :, None] * N_KEYS + idx[:, :, 1, None, :]
    top_val, top_pos = lax.top_k(cand.reshape(T, PEER_HEADS, PEER_TOPK * PEER_TOPK), PEER_TOPK)
    expert = jnp.take_along_axis(cand_idx.reshape(T, PEER_HEADS, -1), top_pos, axis=-1)
    gate = jax.nn.softmax(top_val, axis=-1).astype(y.dtype)
    nb = T // PEER_BLOCK

    def block(args):
        xb, eb, gb = args
        ub = jnp.take(u, eb, axis=0)
        act = gb * jax.nn.gelu(jnp.einsum('thkd,td->thk', ub, xb), approximate=False)
        vb = jnp.take(v, eb, axis=0)
        return jnp.einsum('thk,thkd->td', act, vb)

    out = lax.map(block, (yt.reshape(nb, PEER_BLOCK, D),
                          expert.reshape(nb, PEER_BLOCK, PEER_HEADS, PEER_TOPK),
                          gate.reshape(nb, PEER_BLOCK, PEER_HEADS, PEER_TOPK)))
    return out.reshape(B, L, D)

def setup_inputs(seed: int = 0) -> dict:
    key = jax.random.key(seed)
    ks = jax.random.split(key, 20)
    n = lambda k, shape, s: jax.random.normal(k, shape, jnp.float32) * s
    D = D_MODEL
    return {
        "x": n(ks[0], (BATCH, SEQ, D), 1.0),
        "meta_tokens": n(ks[1], (N_META, D), 1.0),
        "mix_norm_g": 1.0 + n(ks[2], (DEPTH, D), 0.02),
        "ffn_norm_g": 1.0 + n(ks[3], (DEPTH, D), 0.02),
        "final_norm_g": 1.0 + n(ks[4], (D,), 0.02),
        "ab_w_in": n(ks[5], (N_EVEN, D, AB_IN), D ** -0.5),
        "ab_conv_w": n(ks[6], (N_EVEN, B_CONV, B_WIDTH), B_CONV ** -0.5),
        "ab_w_out": n(ks[7], (N_EVEN, MIX_WIDTH, D), MIX_WIDTH ** -0.5),
        "cf_w_pw1": n(ks[8], (N_ODD, D, 2 * CF_INNER), D ** -0.5),
        "cf_b_pw1": n(ks[9], (N_ODD, 2 * CF_INNER), 0.02),
        "cf_conv_w": n(ks[10], (N_ODD, CF_CONV, CF_INNER), CF_CONV ** -0.5),
        "cf_conv_b": n(ks[11], (N_ODD, CF_INNER), 0.02),
        "cf_ln_g": 1.0 + n(ks[12], (N_ODD, CF_INNER), 0.02),
        "cf_ln_b": n(ks[13], (N_ODD, CF_INNER), 0.02),
        "cf_w_pw2": n(ks[14], (N_ODD, CF_INNER, D), CF_INNER ** -0.5),
        "cf_b_pw2": n(ks[15], (N_ODD, D), 0.02),
        "peer_w_q": n(ks[16], (DEPTH, D, PEER_HEADS * PEER_KEY_DIM), D ** -0.5),
        "peer_sub_keys": n(ks[17], (DEPTH, 2, N_KEYS, PEER_HALF), PEER_HALF ** -0.5),
        "peer_u": n(ks[18], (DEPTH, N_EXPERTS, D), D ** -0.5),
        "peer_v": n(ks[19], (DEPTH, N_EXPERTS, D), PEER_HEADS ** -0.5),
    }

def reference(x, meta_tokens, mix_norm_g, ffn_norm_g, final_norm_g, ab_w_in, ab_conv_w,
              ab_w_out, cf_w_pw1, cf_b_pw1, cf_conv_w, cf_conv_b, cf_ln_g, cf_ln_b,
              cf_w_pw2, cf_b_pw2, peer_w_q, peer_sub_keys, peer_u, peer_v):
    B, S, D = x.shape
    L = S + N_META
    Lp = -(-L // BLOCK_Q) * BLOCK_Q
    h = jnp.concatenate([
        jnp.broadcast_to(meta_tokens.astype(x.dtype)[None], (B, N_META, D)),
        x,
        jnp.zeros((B, Lp - L, D), x.dtype)], axis=1)
    for i in range(DEPTH):
        y = rmsnorm(h, mix_norm_g[i])
        if i % 2 == 0:
            j = i // 2
            h = h + mixer_ab(y, ab_w_in[j], ab_conv_w[j], ab_w_out[j])
        else:
            j = i // 2
            h = h + mixer_conformer(y, cf_w_pw1[j], cf_b_pw1[j], cf_conv_w[j], cf_conv_b[j],
                                    cf_ln_g[j], cf_ln_b[j], cf_w_pw2[j], cf_b_pw2[j])
        y = rmsnorm(h, ffn_norm_g[i])
        h = h + peer(y, peer_w_q[i], peer_sub_keys[i], peer_u[i], peer_v[i])
    h = rmsnorm(h, final_norm_g)
    return h[:, N_META:N_META + S, :]


_drawn_inputs = setup_inputs


def setup_inputs(seed=0):
    import zlib

    import numpy as np

    out = dict(_drawn_inputs(seed))
    spreads = {}
    factors = {'final_norm_g': 2.882,
     'cf_b_pw1': 3.456,
     'cf_ln_g': 3.454,
     'cf_ln_b': 3.677,
     'cf_b_pw2': 2.72}
    for name, (base, spread) in spreads.items():
        noise = np.random.default_rng([zlib.crc32(name.encode()), seed]).standard_normal(out[name].shape)
        drawn = base * np.exp(spread * noise) if base else spread * noise
        out[name] = __import__('jax').numpy.asarray(drawn.astype(out[name].dtype))
    for name, factor in factors.items():
        out[name] = (out[name] * factor).astype(out[name].dtype)
    return out
```

```python
import concourse.bass as bass
from concourse import mybir
from contextlib import ExitStack


def hybrid_trunk(nc, x, meta_tokens, mix_norm_g, ffn_norm_g, final_norm_g, ab_w_in, ab_conv_w, ab_w_out,
                 cf_w_pw1, cf_b_pw1, cf_conv_w, cf_conv_b, cf_ln_g, cf_ln_b, cf_w_pw2, cf_b_pw2,
                 peer_w_q, peer_sub_keys, peer_u, peer_v, out):
    f32, u32 = mybir.dt.float32, mybir.dt.uint32
    ALU, ACT = mybir.AluOpType, mybir.ActivationFunctionType
    AX = mybir.AxisListType.X

    P = 128
    D = x.shape[2]
    C = D // P
    META = meta_tokens.shape[0]
    SEQ = x.shape[1]
    L = META + SEQ
    TILES = SEQ // P
    AH = 8
    AW = D // 2
    DH = AW // AH
    AC = AW // P
    KC = ab_conv_w.shape[1]
    CK = cf_conv_w.shape[1]
    H = 8
    NK = peer_sub_keys.shape[2]
    NE = peer_u.shape[1]
    TOPK = 16
    GT = P // H
    EPS = 1e-6
    LOW = -3.0e38
    NB = 4

    KT = [(0, P), (P, P), (2 * P, L - 2 * P)]
    KW = [L - k0 for k0, _ in KT]
    KO = [0, KW[0], KW[0] + KW[1]]
    ZW = sum(KW)

    ctx = ExitStack()
    with ctx:
        def sb(name, shape, dt=f32):
            return ctx.enter_context(nc.sbuf_tensor(name, shape, dt))

        def sem(name):
            return ctx.enter_context(nc.semaphore(name))

        big = sb("big", [P, 32, D])
        rowsU = big[:, 0:TOPK, :]
        rowsV = big[:, TOPK:2 * TOPK, :]
        flat = big[:, :, :].rearrange("p a b -> p (a b)")
        room = [0]

        def carve(*shape):
            n = 1
            for s in shape:
                n *= s
            a = flat[:, room[0]:room[0] + n]
            room[0] += n
            assert room[0] <= 32 * D
            if len(shape) == 1:
                return a
            if len(shape) == 2:
                return a.rearrange("p (a b) -> p a b", b=shape[1])
            return a.rearrange("p (a b c) -> p a b c", b=shape[1], c=shape[2])

        wring = sb("wring", [P, NB, C, P])
        hT = sb("hT", [P, C, L])
        yT = sb("yT", [P, C, L])
        ident = sb("ident", [P, P])
        ones = sb("ones", [P, P])
        tri = sb("tri", [P, P])
        sel = sb("sel", [P, GT])
        iota16 = sb("iota16", [P, TOPK])
        epsc = sb("epsc", [P, 1])
        keysT = sb("keysT", [P, 4, NK])
        convT = sb("convT", [P, C, CK])
        NPAR = 2 * C + 2 * C + C + KC * AC + 2 * C + 5 * C - C
        params = sb("params", [P, NPAR])
        rstd = sb("rstd", [P, L])
        yg = sb("yg", [P, C, H, GT])
        qg = sb("qg", [P, 2, H, GT])
        val = sb("val", [P, 2, TOPK])
        idx = sb("idx", [P, 2, TOPK], u32)
        idxf = sb("idxf", [P, 2, TOPK])
        rest = sb("rest", [P, 2, NK])
        cand = sb("cand", [P, TOPK, TOPK])
        cand2 = sb("cand2", [P, TOPK, TOPK])
        topv = sb("topv", [P, TOPK])
        topp = sb("topp", [P, TOPK], u32)
        posu = sb("posu", [P, 2, TOPK], u32)
        posf = sb("posf", [P, 2, TOPK])
        hot = sb("hot", [P, 2, TOPK, TOPK])
        picked = sb("picked", [P, 2, TOPK])
        expU = sb("expU", [P, TOPK], u32)
        expV = sb("expV", [P, TOPK], u32)
        negm = sb("negm", [P, 1])
        gexp = sb("gexp", [P, TOPK])
        gsum = sb("gsum", [P, 1])
        grec = sb("grec", [P, 1])
        dots = sb("dots", [P, TOPK])
        gel = sb("gel", [P, TOPK])
        coef = sb("coef", [P, TOPK])
        mix = sb("mix", [P, TOPK, GT])
        osb = sb("osb", [GT, D])
        qT = sb("qT", [P, H, 2, L])

        xin = carve(TILES, D)
        min_ = carve(D)
        kin = carve(4, P)
        cin = carve(D)
        pin = carve(P)
        room[0] = 0
        sq = carve(C, L)
        proj = carve(24, L)
        Z = carve(AH, ZW)
        A = carve(AH, ZW)
        S = carve(AH, ZW)
        vtok = carve(3, AW)
        mixT = carve(C, L)
        cx = carve(AC, L + KC - 1)
        ct = carve(AC, L)
        room[0] = C * L
        gz = carve(C, L + CK - 1)
        sg = carve(2, L)
        cv = carve(C, SEQ)
        xc = carve(C, SEQ)
        mu = carve(SEQ)
        sz = carve(C, SEQ)
        yF = carve(C, SEQ)
        outs = carve(TILES, D)

        ps = ctx.enter_context(nc.psum_tensor("ps", [P, 8, 512], f32))
        psn = ps[:, 7, 0:L]
        yrep = ps[:, 2:4, :].rearrange("p a b -> p (a b)")
        psc = ps[:, 4, 0:2 * NK]
        po = ps[:, 5:7, :]
        pt = ps[:, 7, 0:C * GT].rearrange("p (c t) -> p c t", t=GT)

        prow = {}
        loads = []
        n = 0
        for name, ap in (("mix_g", mix_norm_g.rearrange("l (c p) -> (l c) p", p=P)),
                         ("ffn_g", ffn_norm_g.rearrange("l (c p) -> (l c) p", p=P)),
                         ("fin_g", final_norm_g.rearrange("(c p) -> c p", p=P)),
                         ("ab_w", ab_conv_w[0].rearrange("k (c p) -> (k c) p", p=P)),
                         ("pw1_b", cf_b_pw1.rearrange("l (c p) -> (l c) p", p=P)),
                         ("cv_b", cf_conv_b.rearrange("l (c p) -> (l c) p", p=P)),
                         ("ln_g", cf_ln_g.rearrange("l (c p) -> (l c) p", p=P)),
                         ("ln_b", cf_ln_b.rearrange("l (c p) -> (l c) p", p=P)),
                         ("pw2_b", cf_b_pw2.rearrange("l (c p) -> (l c) p", p=P))):
            prow[name] = n
            loads.append((n, ap))
            n += ap.shape[0]
        assert n == NPAR <= P

        def par(name, i):
            return params[:, prow[name] + i:prow[name] + i + 1]

        keys_dram = peer_sub_keys.rearrange("l s n c -> n (l s) c")
        u_rows = peer_u.rearrange("l e d -> (l e) d")
        v_rows = peer_v.rearrange("l e d -> (l e) d")

        s_par = sem("s_par")
        s_x = sem("s_x")
        s_keys = sem("s_keys")
        s_cw = sem("s_cw")
        s_w = [sem(f"s_w{b}") for b in range(NB)]
        s_const = sem("s_const")
        s_pdve = sem("s_pdve")
        s_tp = sem("s_tp")
        s_tpe = sem("s_tpe")
        s_sq = sem("s_sq")
        s_ss = sem("s_ss")
        s_rms = sem("s_rms")
        s_y = sem("s_y")
        s_proj = sem("s_proj")
        s_bank = [sem(f"s_bank{b}") for b in range(2)]
        s_vt = sem("s_vt")
        s_vte = sem("s_vte")
        s_z = sem("s_z")
        s_ze = sem("s_ze")
        s_zz = sem("s_zz")
        s_abs = sem("s_abs")
        s_e0 = sem("s_e0")
        s_ln = sem("s_ln")
        s_spl = sem("s_spl")
        s_spm = sem("s_spm")
        s_suf = sem("s_suf")
        s_lw = sem("s_lw")
        s_ew = sem("s_ew")
        s_wm = sem("s_wm")
        s_av = sem("s_av")
        s_ave = sem("s_ave")
        s_b = sem("s_b")
        s_pad = sem("s_pad")
        s_res = sem("s_res")
        s_sg = sem("s_sg")
        s_gz = sem("s_gz")
        s_cv = sem("s_cv")
        s_mu = sem("s_mu")
        s_xc = sem("s_xc")
        s_xn = sem("s_xn")
        s_sz = sem("s_sz")
        s_chain = sem("s_chain")
        s_qg = sem("s_qg")
        s_yg = sem("s_yg")
        s_sc = sem("s_sc")
        s_yr = sem("s_yr")
        s_top = sem("s_top")
        s_exp = sem("s_exp")
        s_idx = sem("s_idx")
        s_idv = sem("s_idv")
        s_u = [sem(f"s_u{k}") for k in range(TOPK)]
        s_v = [sem(f"s_v{k}") for k in range(TOPK)]
        s_dot = sem("s_dot")
        s_gel = sem("s_gel")
        s_m = sem("s_m")
        s_vm = sem("s_vm")
        s_oe = sem("s_oe")
        s_ot = sem("s_ot")
        s_ha = sem("s_ha")
        s_rdy = sem("s_rdy")
        s_ft = sem("s_ft")
        s_fe = sem("s_fe")
        s_out = sem("s_out")
        s_turn = {e: sem("s_turn_" + e) for e in ("pool", "dve", "act", "pe")}

        def hold(eng, name, s, value):
            eng.wait_ge(s, value)
            eng.sem_inc(s_turn[name], 1)

        w_in, w_out = ab_w_in[0], ab_w_out[0]
        w_pw1, w_pw2 = cf_w_pw1[0], cf_w_pw2[0]
        w_q = [peer_w_q[i] for i in range(2)]
        SEQW = [("in", w_in, 24), ("out", w_out, 8), ("q0", w_q[0], 16), ("pw1", w_pw1, 16), ("pw2", w_pw2, 8),
                ("q1", w_q[1], 16)]
        first = {}
        at = 0
        for name, _, k in SEQW:
            first[name] = at
            at += k
        groups = [L // GT, SEQ // GT]
        gbase = [0, groups[0]]
        toff = [0, META]

        block = ctx.enter_context(nc.Block())

        @block.sync
        def _(sp):
            for r, ap in loads:
                sp.dma_start(pin[r:r + ap.shape[0], :], ap).then_inc(s_par, 16)
            for i in range(TILES):
                sp.dma_start(xin[:, i, :], x[0, i * P:(i + 1) * P, :]).then_inc(s_x, 16)
            sp.dma_start(min_[0:META, :], meta_tokens).then_inc(s_x, 16)
            sp.dma_start(kin, keys_dram).then_inc(s_keys, 16)
            sp.dma_start(cin[0:CK, :], cf_conv_w[0]).then_inc(s_cw, 16)

            def chunk(w, b, col):
                return sp.dma_start(wring[:, b, :, :], w.rearrange("(c p) n -> p c n", p=P)[:, :, col]).then_inc(s_w[b], 16)

            for name, w, k in SEQW:
                for r0 in range(0, k // NB):
                    pass
                if first[name] == 0:
                    for b in range(NB):
                        chunk(w, b, bass.ts(b, P))
                    lo = 1
                else:
                    lo = 0
                with sp.Fori(lo, k // NB) if k // NB - lo > 1 else ExitStack() as r:
                    if k // NB - lo <= 1:
                        r = lo
                    for b in range(NB):
                        sp.wait_ge(s_proj, first[name] + r * NB + b - NB + 1)
                        if name == "pw1":
                            col = bass.ds(r * (NB // 2 * P) + (b % 2) * D + b // 2 * P, P)
                        else:
                            col = bass.ds(r * (NB * P) + b * P, P)
                        chunk(w, b, col)
            sp.wait_ge(s_fe, TILES * 2)
            sp.dma_start(out[0].rearrange("(i p) d -> p i d", p=P), outs).then_inc(s_out, 16)
            sp.wait_ge(s_out, 16)

        @block.gpsimd
        def _(pool):
            nc.gpsimd.memset(ident[:, :], 0.0).then_inc(s_const, 1)
            nc.gpsimd.memset(ones[:, :], 1.0).then_inc(s_const, 1)
            nc.gpsimd.memset(epsc[:, :], EPS).then_inc(s_const, 1)
            nc.gpsimd.iota(iota16[:, :], [[1, TOPK]], base=0, channel_multiplier=0,
                           allow_small_or_imprecise_dtypes=True).then_inc(s_const, 1)
            pool.wait_ge(s_const, 4)
            nc.gpsimd.affine_select(out=ident[:, :], in_=ident[:, :], compare_op=ALU.not_equal, fill=1.0, base=0,
                                    pattern=[[-1, P]], channel_multiplier=1).then_inc(s_const, 1)
            nc.gpsimd.affine_select(out=tri[:, :], in_=ones[:, :], compare_op=ALU.is_ge, fill=0.0, base=0,
                                    pattern=[[-1, P]], channel_multiplier=1).then_inc(s_const, 1)
            pool.wait_ge(s_tpe, 9)
            nc.gpsimd.memset(cx[:, :, 0:KC - 1], 0.0).then_inc(s_pad, 1)
            nc.gpsimd.memset(Z[:, :, KO[2]:ZW], 0.0).then_inc(s_zz, 1)

            def mask(t, half, done):
                for (k0, kn), ko in zip(KT, KO):
                    v = t[0:kn, half * (AH // 2):(half + 1) * (AH // 2), ko:ko + kn]
                    nc.gpsimd.affine_select(out=v, in_=v, compare_op=ALU.is_gt, fill=0.0, base=0,
                                            pattern=[[0, AH // 2], [1, kn]], channel_multiplier=-1).then_inc(done, 1)

            for half in range(2):
                pool.wait_ge(s_spl, half + 1)
                mask(S, half, s_spm)
            for half in range(2):
                pool.wait_ge(s_ew, half + 1)
                mask(A, half, s_wm)

            def gathers(layer, g):
                n = gbase[layer] + g
                hold(pool, "pool", s_idx, n + 1)
                for k in range(TOPK):
                    hold(pool, "pool", s_dot, n * TOPK + k + 1)
                    pool.indirect_dma_start(out=rowsU[:, k, :], out_offset=None, in_=u_rows,
                                            in_offset=bass.IndirectOffsetOnAxis(ap=expU[:, k:k + 1], axis=0)
                                            ).then_inc(s_u[k], 16)
                hold(pool, "pool", s_vm, n * TOPK + 1)
                nc.gpsimd.tensor_copy(expV[:, :], expU[:, :]).then_inc(s_idv, 1)
                hold(pool, "pool", s_idv, n + 2)
                for k in range(TOPK):
                    pool.indirect_dma_start(out=rowsV[:, k, :], out_offset=None, in_=v_rows,
                                            in_offset=bass.IndirectOffsetOnAxis(ap=expV[:, k:k + 1], axis=0)
                                            ).then_inc(s_v[k], 16)

            pool.sem_inc(s_idv, 1)
            pool.wait_ge(s_y, 2)
            with pool.Fori(0, groups[0]) as g:
                gathers(0, g)
            pool.wait_ge(s_vm, 1 + groups[0] * TOPK)
            nc.gpsimd.memset(gz[:, :, 0:CK - 1], 0.0).then_inc(s_pad, 1)
            pool.wait_ge(s_y, 4)
            with pool.Fori(0, groups[1]) as g:
                gathers(1, g)

        @block.scalar
        def _(act):
            act.sem_inc(s_bank[0], 1)
            act.sem_inc(s_bank[1], 1)
            act.sem_inc(s_ha, 1)
            act.sem_inc(s_dot, TOPK)
            act.sem_inc(s_vm, 1)
            act.wait_ge(s_tp, 1)
            act.copy(params[:, :], ps[:, 0, 0:NPAR]).then_inc(s_tpe, 1)
            for i in range(TILES):
                for q in range(2):
                    act.wait_ge(s_tp, 2 + 2 * i + q)
                    act.copy(hT[:, 4 * q:4 * q + 4, META + i * P:META + (i + 1) * P],
                             ps[:, 1 + 2 * i + q, :].rearrange("p (c t) -> p c t", t=P)).then_inc(s_tpe, 1)
            act.wait_ge(s_tp, 6)
            act.copy(hT[:, :, 0:META], ps[:, 5, 0:C * META].rearrange("p (c t) -> p c t", t=META)).then_inc(s_tpe, 1)
            act.wait_ge(s_tp, 7)
            act.copy(keysT[:, :, :], ps[:, 6, :].rearrange("p (s k) -> p s k", k=NK)).then_inc(s_tpe, 1)
            act.wait_ge(s_tp, 8)
            act.copy(convT[:, :, :], ps[:, 7, 0:C * CK].rearrange("p (c k) -> p c k", k=CK)).then_inc(s_tpe, 1)
            act.wait_ge(s_tpe, 8)
            act.sem_inc(s_tpe, 1)

            nn = [0]

            def norm(src, w):
                act.activation(sq[:, :, 0:w], src, ACT.Square).then_inc(s_sq, 1)
                act.wait_ge(s_ss, nn[0] + 1)
                act.activation(rstd[:, 0:w], psn[:, 0:w], ACT.Sqrt, bias=epsc[:, :], scale=1.0 / D).then_inc(s_rms, 1)
                nn[0] += 1

            def evacuate(name, count, dst):
                n0 = first[name]
                with act.Fori(0, count // NB) as r:
                    for b in range(NB):
                        hold(act, "act", s_proj, n0 + r * NB + b + 1)
                        act.copy(dst(r, b), ps[:, b % 2, 0:L]).then_inc(s_bank[b % 2], 1)

            norm(hT[:, :, :], L)
            evacuate("in", 24, lambda r, b: proj[:, bass.ds(r * NB + b, 1), :].rearrange("p a t -> p (a t)"))
            act.wait_ge(s_zz, 1)
            for h in range(AH):
                act.wait_ge(s_z, h + 1)
                b = 2 + h % 6
                act.activation(Z[:, h, 0:KO[2]], ps[:, b, 0:KO[2]], ACT.Copy, scale=DH ** -0.5).then_inc(s_ze, 1)
                act.activation(Z[0:KT[2][1], h, KO[2]:ZW], ps[0:KT[2][1], b, KO[2]:ZW], ACT.Copy,
                               scale=DH ** -0.5).then_inc(s_ze, 1)
            HH = AH // 2
            for half in range(2):
                a = A[:, half * HH:(half + 1) * HH, :]
                act.wait_ge(s_ze, (half + 1) * AH)
                act.activation(a, Z[:, half * HH:(half + 1) * HH, :], ACT.Abs).then_inc(s_abs, 1)
                act.wait_ge(s_abs, half + 1)
                act.activation(a, a, ACT.Exp, scale=-1.0).then_inc(s_e0, 1)
                act.wait_ge(s_e0, half + 1)
                act.activation(a, a, ACT.Ln, bias=1.0).then_inc(s_ln, 1)
            for half in range(2):
                act.wait_ge(s_lw, (half + 1) * AH)
                act.activation(A[:, half * HH:(half + 1) * HH, :], Z[:, half * HH:(half + 1) * HH, :],
                               ACT.Exp).then_inc(s_ew, 1)
            for c in range(AC):
                act.wait_ge(s_av, 2 * c + 2)
                act.copy(mixT[:, c, :], ps[:, 2 + c, 0:L]).then_inc(s_ave, 1)

            def peer(layer):
                t0, w, G, base = toff[layer], L - toff[layer], groups[layer], gbase[layer]
                norm(hT[:, :, t0:L], w)
                n0 = first["q%d" % layer]
                with act.Fori(0, 16 // NB) as r:
                    for b in range(NB):
                        hold(act, "act", s_proj, n0 + r * NB + b + 1)
                        act.copy(qT[:, bass.ds(r * (NB // 2) + b // 2, 1), b % 2, t0:L].rearrange("p a t -> p (a t)"),
                                 ps[:, b % 2, 0:w]).then_inc(s_bank[b % 2], 1)

                def prepare(g):
                    n = base + g
                    if isinstance(g, int) and g == 0:
                        act.wait_ge(s_bank[0], 1 + (n0 + 16) // 2)
                        act.wait_ge(s_bank[1], 1 + (n0 + 16) // 2)
                        if layer:
                            act.wait_ge(s_sc, n)
                            act.wait_ge(s_yr, n)
                    else:
                        hold(act, "act", s_sc, n)
                    act.copy(qg[:, :, :, :], qT[:, :, :, bass.ds(t0 + g * GT, GT)].rearrange("p h s t -> p s h t")
                             ).then_inc(s_qg, 1)
                    if not (isinstance(g, int) and g == 0):
                        hold(act, "act", s_yr, n)
                    for h in range(H):
                        act.copy(yg[:, :, h, :], yT[:, :, bass.ds(t0 + g * GT, GT)]).then_inc(s_yg, 1)

                def exps(g):
                    hold(act, "act", s_top, base + g + 1)
                    act.activation(gexp[:, :], topv[:, :], ACT.Exp, bias=negm[:, :], accum_out=gsum[:, :]
                                   ).then_inc(s_exp, 1)

                def body(g, before, after):
                    n = base + g
                    if before:
                        hold(act, "act", s_vm, 1 + n * TOPK)
                        hold(act, "act", s_ot, n - 1) if not isinstance(g, int) or n > 1 else None
                        act.copy(osb[:, :], po[0:GT, :, :].rearrange("p a b -> p (a b)")).then_inc(s_oe, 1)
                    if after:
                        prepare(g + 1)
                    hold(act, "act", s_dot, (n + 2) * TOPK)
                    act.activation(gel[:, :], dots[:, :], ACT.Gelu).then_inc(s_gel, 1)
                    if after:
                        exps(g + 1)

                prepare(0)
                exps(0)
                body(0, False, True)
                body(1, True, True)
                with act.Fori(2, G - 1) as g:
                    body(g, True, True)
                body(G - 1, True, False)
                act.wait_ge(s_vm, 1 + (base + G) * TOPK)
                act.wait_ge(s_ot, base + G - 1)
                act.copy(osb[:, :], po[0:GT, :, :].rearrange("p a b -> p (a b)")).then_inc(s_oe, 1)

            act.wait_ge(s_res, C)
            peer(0)

            act.wait_ge(s_ha, 1 + groups[0])
            norm(hT[:, :, :], L)
            for c in range(C):
                act.wait_ge(s_proj, first["pw1"] + 2 * c + 2)
                if c >= 2:
                    act.wait_ge(s_gz, c - 1)
                act.activation(sg[:, c % 2, :], ps[:, 1, 0:L], ACT.Sigmoid, bias=par("pw1_b", C + c)).then_inc(s_sg, 1)
                act.wait_ge(s_sg, c + 1)
                act.sem_inc(s_bank[1], 1)
            act.wait_ge(s_xc, 1)
            act.activation(sq[:, :, 0:SEQ], xc, ACT.Square).then_inc(s_sq, 1)
            act.wait_ge(s_ss, nn[0] + 1)
            act.activation(rstd[:, 0:SEQ], psn[:, 0:SEQ], ACT.Sqrt, bias=epsc[:, :], scale=1.0 / D).then_inc(s_rms, 1)
            nn[0] += 1
            act.wait_ge(s_xn, 1)
            for c in range(C):
                act.activation(sz[:, c, :], xc[:, c, :], ACT.Silu, bias=par("ln_b", c), scale=par("ln_g", c)
                               ).then_inc(s_sz, 1)
            act.wait_ge(s_res, 2 * C)
            peer(1)

            act.wait_ge(s_ha, 1 + groups[0] + groups[1])
            norm(hT[:, :, META:L], SEQ)
            for i in range(TILES):
                for q in range(2):
                    act.wait_ge(s_ft, 2 * i + q + 1)
                    act.copy(outs[:, i, 512 * q:512 * (q + 1)], ps[:, 2 * i + q, :]).then_inc(s_fe, 1)

        @block.tensor
        def _(pe):
            pe.wait_ge(s_const, 6)
            pe.wait_ge(s_par, 16 * len(loads))
            pe.transpose(ps[:, 0, 0:NPAR], pin[0:NPAR, :], ident[0:NPAR, 0:NPAR]).then_inc(s_tp, 1)
            pe.wait_ge(s_x, 16 * (TILES + 1))
            for i in range(TILES):
                for q in range(2):
                    for c in range(4):
                        last = pe.transpose(ps[:, 1 + 2 * i + q, c * P:(c + 1) * P],
                                            xin[:, i, (4 * q + c) * P:(4 * q + c + 1) * P], ident[:, :])
                    last.then_inc(s_tp, 1)
            for c in range(C):
                last = pe.transpose(ps[:, 5, c * META:(c + 1) * META], min_[0:META, c * P:(c + 1) * P],
                                    ident[0:META, 0:META])
            last.then_inc(s_tp, 1)
            pe.wait_ge(s_keys, 16)
            for s in range(4):
                last = pe.transpose(ps[:, 6, s * NK:(s + 1) * NK], kin[:, s, :], ident[:, :])
            last.then_inc(s_tp, 1)
            pe.wait_ge(s_cw, 16)
            for c in range(C):
                last = pe.transpose(ps[:, 7, c * CK:(c + 1) * CK], cin[0:CK, c * P:(c + 1) * P], ident[0:CK, 0:CK])
            last.then_inc(s_tp, 1)
            pe.wait_ge(s_tpe, 9)

            nn = [0]

            def sums(src, w, s, ready, bank):
                pe.wait_ge(ready[0], ready[1])
                for c in range(C):
                    last = pe.matmul(bank[:, 0:w], ones[:, :], src[:, c, 0:w], start=(c == 0), stop=(c == C - 1))
                last.then_inc(s, 1)

            def norm(w):
                nn[0] += 1
                sums(sq, w, s_ss, (s_sq, nn[0]), psn)

            def chunk(n, r, b, rhs, w):
                pe.wait_ge(s_w[b], 16 * (n + r) + 16)
                pe.wait_ge(s_bank[b % 2], (n + r) * (NB // 2) + b // 2 + 1)
                for c in range(C):
                    last = pe.matmul(ps[:, b % 2, 0:w], wring[:, b, c, :], rhs(c), start=(c == 0), stop=(c == C - 1))
                last.then_inc(s_proj, 1)

            def project(name, count, rhs, w):
                n = first[name] // NB
                if count == NB:
                    for b in range(NB):
                        chunk(n, 0, b, rhs, w)
                else:
                    with pe.Fori(0, count // NB) as r:
                        for b in range(NB):
                            chunk(n, r, b, rhs, w)

            norm(L)
            pe.wait_ge(s_y, 1)
            project("in", 24, lambda c: yT[:, c, :], L)

            pe.wait_ge(s_bank[0], 1 + 12)
            pe.wait_ge(s_bank[1], 1 + 12)
            for t, (k0, kn) in enumerate(KT):
                for c in range(AC):
                    last = pe.transpose(ps[0:kn, 5 + t, c * P:(c + 1) * P], proj[:, 2 * AC + c, k0:k0 + kn], ident[:, :])
                last.then_inc(s_vt, 1)
            for h in range(AH):
                c, q0 = h // 2, DH * (h % 2)
                if h == 3:
                    pe.wait_ge(s_vte, 3)
                if h >= 6:
                    pe.wait_ge(s_ze, 2 * (h - 5))
                for (k0, kn), ko, kw in zip(KT, KO, KW):
                    last = pe.matmul(ps[0:kn, 2 + h % 6, ko:ko + kw], proj[q0:q0 + DH, AC + c, k0:k0 + kn],
                                     proj[q0:q0 + DH, c, k0:L], start=True, stop=True)
                last.then_inc(s_z, 1)
            for h in range(AH):
                if h == 0:
                    pe.wait_ge(s_ze, 2 * AH)
                if h % (AH // 2) == 0:
                    pe.wait_ge(s_spm, 3 * (h // (AH // 2) + 1))
                b = 2 + h % 6
                if h >= 6:
                    pe.wait_ge(s_lw, 2 * (h - 5))
                for i, ((k0, kn), ko, kw) in enumerate(zip(KT, KO, KW)):
                    for j in range(i, 3):
                        (j0, jn), jo, jw = KT[j], KO[j], KW[j]
                        d = j0 - k0
                        last = pe.matmul(ps[0:kn, b, ko + d:ko + kw], (tri if i == j else ones)[0:jn, 0:kn],
                                         S[0:jn, h, jo:jo + jw], start=(j == i), stop=(j == 2))
                last.then_inc(s_suf, 1)
            for h in range(AH):
                if h == 0:
                    pe.wait_ge(s_lw, 2 * AH)
                if h % (AH // 2) == 0:
                    pe.wait_ge(s_wm, 3 * (h // (AH // 2) + 1))
                c, q0 = h // 2, DH * (h % 2)
                for j in range(3):
                    (j0, jn), jo, jw = KT[j], KO[j], KW[j]
                    last = pe.matmul(ps[q0:q0 + DH, 2 + c, j0:L], vtok[0:jn, j, h * DH:(h + 1) * DH],
                                     A[0:jn, h, jo:jo + jw], start=(j == 0), stop=(j == 2))
                last.then_inc(s_av, 1)
            pe.wait_ge(s_ave, AC)
            pe.wait_ge(s_b, AC)
            project("out", 8, lambda c: mixT[:, c, :], L)

            def peer(layer):
                t0, w, G, base = toff[layer], L - toff[layer], groups[layer], gbase[layer]
                norm(w)
                pe.wait_ge(s_y, 2 + 2 * layer)
                project("q%d" % layer, 16, lambda c: yT[:, c, t0:L], w)

                def scores(g):
                    n = base + g
                    hold(pe, "pe", s_qg, n + 1)
                    hold(pe, "pe", s_top, n) if not isinstance(g, int) or n else None
                    for s in range(2):
                        last = pe.matmul(psc[:, s * NK:(s + 1) * NK], qg[:, s, :, :].rearrange("p h t -> p (h t)"),
                                         keysT[:, 2 * layer + s, :], start=True, stop=True)
                    last.then_inc(s_sc, 1)

                def rows(g):
                    n = base + g
                    hold(pe, "pe", s_yg, H * (n + 1))
                    hold(pe, "pe", s_dot, (n + 1) * TOPK)
                    for c in range(C):
                        last = pe.transpose(yrep[:, c * P:(c + 1) * P], yg[:, c, :, :].rearrange("p h t -> p (h t)"),
                                            ident[:, :])
                    last.then_inc(s_yr, 1)

                def values(g):
                    n = base + g
                    hold(pe, "pe", s_m, n + 1)
                    hold(pe, "pe", s_oe, n) if not isinstance(g, int) or n else None
                    for k in range(TOPK):
                        hold(pe, "pe", s_v[k], 16 * (n + 1))
                        for q in range(2):
                            last = pe.matmul(po[0:GT, q, :], mix[:, k, :], rowsV[:, k, 512 * q:512 * (q + 1)],
                                             start=(k == 0), stop=(k == TOPK - 1))
                        last.then_inc(s_vm, 1)

                def back(g):
                    n = base + g
                    hold(pe, "pe", s_oe, n + 1)
                    hold(pe, "pe", s_ha, n + 1)
                    for c in range(C):
                        last = pe.transpose(pt[:, c, :], osb[:, c * P:(c + 1) * P], ident[0:GT, 0:GT])
                    last.then_inc(s_ot, 1)

                def body(g, before, after):
                    if before:
                        back(g - 1)
                    if after:
                        scores(g + 1)
                        rows(g + 1)
                    values(g)

                scores(0)
                rows(0)
                body(0, False, True)
                body(1, True, True)
                with pe.Fori(2, G - 1) as g:
                    body(g, True, True)
                body(G - 1, True, False)
                back(G - 1)

            peer(0)

            norm(L)
            pe.wait_ge(s_y, 3)
            project("pw1", 16, lambda c: yT[:, c, :], L)
            sums(cv, SEQ, s_mu, (s_cv, C), ps[:, 2, :])
            norm(SEQ)
            pe.wait_ge(s_sz, C)
            project("pw2", 8, lambda c: sz[:, c, :], SEQ)
            peer(1)

            norm(SEQ)
            pe.wait_ge(s_rdy, 1)
            for i in range(TILES):
                for q in range(2):
                    for c in range(4):
                        last = pe.transpose(ps[:, 2 * i + q, c * P:(c + 1) * P], yF[:, 4 * q + c, i * P:(i + 1) * P],
                                            ident[:, :])
                    last.then_inc(s_ft, 1)

        @block.vector
        def _(dve):
            chain = [0]

            def link(ins):
                chain[0] += 1
                ins.then_inc(s_chain, 1)
                dve.wait_ge(s_chain, chain[0])

            def norm(m, dst, src, gains, w, done):
                dve.wait_ge(s_rms, m)
                link(nc.vector.reciprocal(rstd[:, 0:w], rstd[:, 0:w]))
                for c in range(C):
                    last = nc.vector.scalar_tensor_tensor(out=dst[:, c, :], in0=src[:, c, :], scalar=par(gains[0], gains[1] + c),
                                                          in1=rstd[:, 0:w], op0=ALU.mult, op1=ALU.mult)
                last.then_inc(done, 1)

            dve.wait_ge(s_const, 6)
            nc.vector.tensor_reduce(out=sel[:, :], in_=ident[:, :].rearrange("p (h t) -> p t h", t=GT), axis=AX,
                                    op=ALU.add).then_inc(s_pdve, 1)
            dve.wait_ge(s_tpe, 9)
            norm(1, yT[:, :, :], hT[:, :, :], ("mix_g", 0), L, s_y)

            for t, (k0, kn) in enumerate(KT):
                dve.wait_ge(s_vt, t + 1)
                nc.vector.tensor_copy(vtok[0:kn, t, :], ps[0:kn, 5 + t, :]).then_inc(s_vte, 1)
            HH = AH // 2
            dve.wait_ge(s_pad, 1)
            link(nc.vector.tensor_tensor(cx[:, :, KC - 1:], proj[:, 4 * AC:5 * AC, :], proj[:, 5 * AC:6 * AC, :], ALU.mult))
            for c in range(AC):
                nc.vector.tensor_scalar(ct[:, c, :], cx[:, c, 0:L], par("ab_w", c), None, ALU.mult).then_inc(s_chain, 1)
                chain[0] += 1
            for k in range(1, KC):
                for c in range(AC):
                    dve.wait_ge(s_chain, chain[0] - AC + 1)
                    nc.vector.scalar_tensor_tensor(out=ct[:, c, :], in0=cx[:, c, k:k + L], scalar=par("ab_w", k * AC + c),
                                                   in1=ct[:, c, :], op0=ALU.mult, op1=ALU.add).then_inc(s_chain, 1)
                    chain[0] += 1
            for half in range(2):
                sl = slice(half * HH, (half + 1) * HH)
                dve.wait_ge(s_ln, half + 1)
                nc.vector.scalar_tensor_tensor(out=S[:, sl, :].rearrange("p a b -> p (a b)"),
                                               in0=Z[:, sl, :].rearrange("p a b -> p (a b)"), scalar=0.0,
                                               in1=A[:, sl, :].rearrange("p a b -> p (a b)"), op0=ALU.max,
                                               op1=ALU.add).then_inc(s_spl, 1)
            for c in range(AC):
                dve.wait_ge(s_chain, chain[0] - AC + 1 + c)
                nc.vector.tensor_tensor(mixT[:, AC + c, :], proj[:, 3 * AC + c, :], ct[:, c, :], ALU.mult).then_inc(s_b, 1)
            for h in range(AH):
                dve.wait_ge(s_suf, h + 1)
                b = 2 + h % 6
                nc.vector.tensor_tensor(Z[:, h, 0:KO[2]], Z[:, h, 0:KO[2]], ps[:, b, 0:KO[2]], ALU.subtract).then_inc(s_lw, 1)
                z2 = Z[0:KT[2][1], h, KO[2]:ZW]
                nc.vector.tensor_tensor(z2, z2, ps[0:KT[2][1], b, KO[2]:ZW], ALU.subtract).then_inc(s_lw, 1)
            for c in range(C):
                dve.wait_ge(s_proj, first["out"] + c + 1)
                nc.vector.tensor_tensor(hT[:, c, :], hT[:, c, :], ps[:, c % 2, 0:L], ALU.add).then_inc(s_res, 1)
                dve.wait_ge(s_res, c + 1)
                dve.sem_inc(s_bank[c % 2], 1)

            def peer(layer):
                t0, w, G, base = toff[layer], L - toff[layer], groups[layer], gbase[layer]

                def route(g):
                    n = base + g
                    hold(dve, "dve", s_sc, n + 1)
                    sc = [psc[:, s * NK:(s + 1) * NK] for s in range(2)]
                    for s in range(2):
                        nc.vector.max(val[:, s, 0:8], sc[s])
                    dve.drain()
                    for s in range(2):
                        nc.vector.max_index(idx[:, s, 0:8], val[:, s, 0:8], sc[s])
                        nc.vector.match_replace(rest[:, s, :], val[:, s, 0:8], sc[s], LOW)
                    dve.drain()
                    for s in range(2):
                        nc.vector.max(val[:, s, 8:16], rest[:, s, :])
                    dve.drain()
                    for s in range(2):
                        nc.vector.max_index(idx[:, s, 8:16], val[:, s, 8:16], rest[:, s, :])
                    nc.vector.tensor_tensor(cand[:, :, :], val[:, 0, :].unsqueeze(2).to_broadcast([P, TOPK, TOPK]),
                                            val[:, 1, :].unsqueeze(1).to_broadcast([P, TOPK, TOPK]), ALU.add)
                    dve.drain()
                    c1 = cand[:, :, :].rearrange("p a b -> p (a b)")
                    c2 = cand2[:, :, :].rearrange("p a b -> p (a b)")
                    nc.vector.max(topv[:, 0:8], c1)
                    nc.vector.tensor_scalar(idxf[:, 0, :], idx[:, 0, :], float(NK), None, ALU.mult)
                    nc.vector.tensor_scalar(idxf[:, 1, :], idx[:, 1, :], float(layer * NE), None, ALU.add)
                    dve.drain()
                    nc.vector.max_index(topp[:, 0:8], topv[:, 0:8], c1)
                    nc.vector.match_replace(c2, topv[:, 0:8], c1, LOW)
                    nc.vector.tensor_scalar(negm[:, :], topv[:, 0:1], -1.0, None, ALU.mult)
                    dve.drain()
                    nc.vector.max(topv[:, 8:16], c2).then_inc(s_top, 1)
                    dve.drain()
                    nc.vector.max_index(topp[:, 8:16], topv[:, 8:16], c2)
                    dve.drain()
                    nc.vector.tensor_scalar(posu[:, 0, :], topp[:, :], 4, None, ALU.logical_shift_right)
                    nc.vector.tensor_scalar(posu[:, 1, :], topp[:, :], 15, None, ALU.bitwise_and)
                    dve.drain()
                    nc.vector.tensor_copy(posf[:, :, :], posu[:, :, :])
                    dve.drain()
                    for s in range(2):
                        nc.vector.tensor_tensor(hot[:, s, :, :], posf[:, s, :].unsqueeze(2).to_broadcast([P, TOPK, TOPK]),
                                                iota16[:, :].unsqueeze(1).to_broadcast([P, TOPK, TOPK]), ALU.is_equal)
                    dve.drain()
                    for s in range(2):
                        nc.vector.tensor_tensor(hot[:, s, :, :], hot[:, s, :, :],
                                                idxf[:, s, :].unsqueeze(1).to_broadcast([P, TOPK, TOPK]), ALU.mult)
                    dve.drain()
                    nc.vector.tensor_reduce(out=picked[:, :, :], in_=hot[:, :, :, :], axis=AX, op=ALU.add)
                    dve.drain()
                    hold(dve, "dve", s_idv, n + 1)
                    nc.vector.tensor_tensor(expU[:, :], picked[:, 0, :], picked[:, 1, :], ALU.add).then_inc(s_idx, 1)

                def body(g, before, after):
                    n = base + g
                    hold(dve, "dve", s_yr, n + 1)
                    hold(dve, "dve", s_gel, n) if not isinstance(g, int) or n else None
                    for k in range(TOPK):
                        hold(dve, "dve", s_u[k], 16 * (n + 1))
                        nc.vector.tensor_tensor_reduce(out=rowsU[:, k, :], in0=rowsU[:, k, :], in1=yrep, scale=1.0,
                                                       scalar=0.0, op0=ALU.mult, op1=ALU.add,
                                                       accum_out=dots[:, k:k + 1]).then_inc(s_dot, 1)
                    hold(dve, "dve", s_exp, n + 1)
                    nc.vector.reciprocal(grec[:, :], gsum[:, :])
                    hold(dve, "dve", s_gel, n + 1)
                    dve.drain()
                    nc.vector.scalar_tensor_tensor(out=coef[:, :], in0=gel[:, :], scalar=grec[:, :], in1=gexp[:, :],
                                                   op0=ALU.mult, op1=ALU.mult)
                    hold(dve, "dve", s_vm, 1 + n * TOPK)
                    dve.drain()
                    nc.vector.tensor_tensor(mix[:, :, :], coef[:, :].unsqueeze(2).to_broadcast([P, TOPK, GT]),
                                            sel[:, :].unsqueeze(1).to_broadcast([P, TOPK, GT]), ALU.mult).then_inc(s_m, 1)
                    if after:
                        route(g + 1)
                    if before:
                        add_back(g - 1)

                def add_back(g):
                    hold(dve, "dve", s_ot, base + g + 1)
                    hv = hT[:, :, bass.ds(t0 + g * GT, GT)]
                    nc.vector.tensor_tensor(hv, hv, pt, ALU.add).then_inc(s_ha, 1)

                dve.wait_ge(s_pdve, 1)
                route(0)
                body(0, False, True)
                body(1, True, True)
                with dve.Fori(2, G - 1) as g:
                    body(g, True, True)
                body(G - 1, True, False)
                add_back(G - 1)

            norm(2, yT[:, :, :], hT[:, :, :], ("ffn_g", 0), L, s_y)
            peer(0)

            norm(3, yT[:, :, :], hT[:, :, :], ("mix_g", C), L, s_y)
            dve.wait_ge(s_pad, 2)
            for c in range(C):
                dve.wait_ge(s_sg, c + 1)
                nc.vector.scalar_tensor_tensor(out=gz[:, c, CK - 1:], in0=ps[:, 0, 0:L], scalar=par("pw1_b", c),
                                               in1=sg[:, c % 2, :], op0=ALU.add, op1=ALU.mult).then_inc(s_gz, 1)
                dve.wait_ge(s_gz, c + 1)
                dve.sem_inc(s_bank[0], 1)
                link(nc.vector.tensor_scalar(cv[:, c, :], gz[:, c, META:META + SEQ], convT[:, c, 0:1], par("cv_b", c),
                                             ALU.mult, ALU.add))
                for k in range(1, CK):
                    ins = nc.vector.scalar_tensor_tensor(out=cv[:, c, :], in0=gz[:, c, META + k:META + k + SEQ],
                                                         scalar=convT[:, c, k:k + 1], in1=cv[:, c, :], op0=ALU.mult,
                                                         op1=ALU.add)
                    if k < CK - 1:
                        link(ins)
                    else:
                        ins.then_inc(s_cv, 1)
            dve.wait_ge(s_cv, C)
            dve.wait_ge(s_mu, 1)
            link(nc.vector.tensor_scalar(mu, ps[:, 2, 0:SEQ], 1.0 / D, None, ALU.mult))
            nc.vector.tensor_tensor(xc, cv, mu.unsqueeze(1).to_broadcast([P, C, SEQ]), ALU.subtract).then_inc(s_xc, 1)
            dve.wait_ge(s_rms, 4)
            link(nc.vector.reciprocal(rstd[:, 0:SEQ], rstd[:, 0:SEQ]))
            nc.vector.tensor_tensor(xc, xc, rstd[:, 0:SEQ].unsqueeze(1).to_broadcast([P, C, SEQ]), ALU.mult).then_inc(s_xn, 1)
            for c in range(C):
                dve.wait_ge(s_proj, first["pw2"] + c + 1)
                nc.vector.scalar_tensor_tensor(out=hT[:, c, META:L], in0=ps[:, c % 2, 0:SEQ], scalar=par("pw2_b", c),
                                               in1=hT[:, c, META:L], op0=ALU.add, op1=ALU.add).then_inc(s_res, 1)
                dve.wait_ge(s_res, C + c + 1)
                dve.sem_inc(s_bank[c % 2], 1)
            norm(5, yT[:, :, META:L], hT[:, :, META:L], ("ffn_g", C), SEQ, s_y)
            peer(1)
            norm(6, yF, hT[:, :, META:L], ("fin_g", 0), SEQ, s_rdy)


_INS = ['x', 'meta_tokens', 'mix_norm_g', 'ffn_norm_g', 'final_norm_g', 'ab_w_in', 'ab_conv_w', 'ab_w_out', 'cf_w_pw1',
        'cf_b_pw1', 'cf_conv_w', 'cf_conv_b', 'cf_ln_g', 'cf_ln_b', 'cf_w_pw2', 'cf_b_pw2', 'peer_w_q',
        'peer_sub_keys', 'peer_u', 'peer_v']


def kernel(**inputs):
    import numpy as _np
    import concourse.bacc as _bacc
    from concourse import mybir as _mybir
    from concourse.bass_utils import run_bass_kernel_spmd as _run

    nc = _bacc.Bacc("TRN2", target_bir_lowering=False, num_devices=1)
    arrays, args = {}, []
    for name in _INS:
        a = _np.ascontiguousarray(inputs[name])
        arrays[f"in_{name}_dram"] = a
        args.append(nc.dram_tensor(f"in_{name}_dram", a.shape, _mybir.dt.from_np(a.dtype), kind="ExternalInput").ap())
    shape = tuple(inputs["x"].shape)
    args.append(nc.dram_tensor("out_0_dram", shape, _mybir.dt.float32, kind="ExternalOutput").ap())
    hybrid_trunk(nc, *args)
    r = _run(nc, [arrays], core_ids=[0])
    return r.results[0]["out_0_dram"]
```

```python
import concourse.bass as bass
from concourse import mybir
from contextlib import ExitStack


def hybrid_trunk(nc, x, meta_tokens, mix_norm_g, ffn_norm_g, final_norm_g, ab_w_in, ab_conv_w, ab_w_out,
                 cf_w_pw1, cf_b_pw1, cf_conv_w, cf_conv_b, cf_ln_g, cf_ln_b, cf_w_pw2, cf_b_pw2,
                 peer_w_q, peer_sub_keys, peer_u, peer_v, out):
    f32, u32 = mybir.dt.float32, mybir.dt.uint32
    ALU, ACT = mybir.AluOpType, mybir.ActivationFunctionType
    AX = mybir.AxisListType.X

    P = 128
    D = x.shape[2]
    C = D // P
    META = meta_tokens.shape[0]
    SEQ = x.shape[1]
    L = META + SEQ
    TILES = SEQ // P
    AH = 8
    AW = D // 2
    DH = AW // AH
    AC = AW // P
    KC = ab_conv_w.shape[1]
    CK = cf_conv_w.shape[1]
    H = 8
    NK = peer_sub_keys.shape[2]
    NE = peer_u.shape[1]
    TOPK = 16
    GT = P // H
    EPS = 1e-6
    LOW = -3.0e38
    NB = 4
    NU = 8

    KT = [(0, P), (P, P), (2 * P, L - 2 * P)]
    KW = [L - k0 for k0, _ in KT]
    KO = [0, KW[0], KW[0] + KW[1]]
    ZW = sum(KW)

    ctx = ExitStack()
    with ctx:
        def sb(name, shape, dt=f32):
            return ctx.enter_context(nc.sbuf_tensor(name, shape, dt))

        def sem(name):
            return ctx.enter_context(nc.semaphore(name))

        big = sb("big", [P, NU + TOPK, D])
        rowsU = big[:, 0:NU, :]
        rowsV = big[:, NU:NU + TOPK, :]
        flat = big[:, :, :].rearrange("p a b -> p (a b)")
        room = [0]

        def carve(*shape):
            n = 1
            for s in shape:
                n *= s
            a = flat[:, room[0]:room[0] + n]
            room[0] += n
            assert room[0] <= (NU + TOPK) * D
            if len(shape) == 1:
                return a
            if len(shape) == 2:
                return a.rearrange("p (a b) -> p a b", b=shape[1])
            return a.rearrange("p (a b c) -> p a b c", b=shape[1], c=shape[2])

        wring = sb("wring", [P, NB, C, P])
        hT = sb("hT", [P, C, L])
        yT = sb("yT", [P, C, L])
        ident = sb("ident", [P, P])
        ones = sb("ones", [P, P])
        tri = sb("tri", [P, P])
        sel = sb("sel", [P, GT])
        iota16 = sb("iota16", [P, TOPK])
        epsc = sb("epsc", [P, 1])
        keysT = sb("keysT", [P, 4, NK])
        convT = sb("convT", [P, C, CK])
        NPAR = 2 * C + 2 * C + C + KC * AC + 2 * C + 5 * C - C
        params = sb("params", [P, NPAR])
        rstd = sb("rstd", [P, L])
        yg = sb("yg", [P, C, H, GT])
        qg = sb("qg", [P, 2, H, GT])
        val = sb("val", [P, 2, TOPK])
        idx = sb("idx", [P, 2, TOPK], u32)
        idxf = sb("idxf", [P, 2, TOPK])
        rest = sb("rest", [P, 2, NK])
        cand = sb("cand", [P, TOPK, TOPK])
        cand2 = sb("cand2", [P, TOPK, TOPK])
        topv = sb("topv", [P, TOPK])
        topp = sb("topp", [P, TOPK], u32)
        posu = sb("posu", [P, 2, TOPK], u32)
        posf = sb("posf", [P, 2, TOPK])
        hot = sb("hot", [P, 2, TOPK, TOPK])
        picked = sb("picked", [P, 2, TOPK])
        expU = sb("expU", [P, TOPK], u32)
        expV = sb("expV", [P, TOPK], u32)
        negm = sb("negm", [P, 1])
        gexp = sb("gexp", [P, TOPK])
        gsum = sb("gsum", [P, 1])
        grec = sb("grec", [P, 1])
        dots = sb("dots", [P, TOPK])
        gel = sb("gel", [P, TOPK])
        coef = sb("coef", [P, TOPK])
        mix = sb("mix", [P, TOPK, GT])
        osb = sb("osb", [GT, D])
        qT = sb("qT", [P, H, 2, L])

        BLOCKS = [(0, L - P, META), (L - P, P, L - P)]
        BW = L - P
        sqb = sb("sqb", [P, C, BW])
        gz = sb("gz", [P, C, L + CK - 1])
        ga = sb("ga", [P, C // 2, BW])
        sg = sb("sg", [P, C // 2, BW])
        cv = sb("cv", [P, C, P])
        mu = sb("mu", [P, P])

        xin = carve(TILES, D)
        min_ = carve(D)
        kin = carve(4, P)
        cin = carve(D)
        pin = carve(P)
        room[0] = 0
        sq = carve(C, L)
        proj = carve(24, L)
        Z = carve(AH, ZW)
        A = carve(AH, ZW)
        S = carve(AH, ZW)
        mixT = carve(C, L)
        cx = carve(AC, L + KC - 1)
        ct = carve(AC, L)
        room[0] = 0
        vtok = carve(3, AW)
        room[0] = C * L
        yF = carve(C, SEQ)
        outs = carve(TILES, D)

        ps = ctx.enter_context(nc.psum_tensor("ps", [P, 8, 512], f32))
        yrep = ps[:, 2:4, :].rearrange("p a b -> p (a b)")
        psc = ps[:, 4, 0:2 * NK]
        po = ps[:, 5:7, :]
        pt = ps[:, 7, 0:C * GT].rearrange("p (c t) -> p c t", t=GT)

        prow = {}
        loads = []
        n = 0
        for name, ap in (("mix_g", mix_norm_g.rearrange("l (c p) -> (l c) p", p=P)),
                         ("ffn_g", ffn_norm_g.rearrange("l (c p) -> (l c) p", p=P)),
                         ("fin_g", final_norm_g.rearrange("(c p) -> c p", p=P)),
                         ("ab_w", ab_conv_w[0].rearrange("k (c p) -> (k c) p", p=P)),
                         ("pw1_b", cf_b_pw1.rearrange("l (c p) -> (l c) p", p=P)),
                         ("cv_b", cf_conv_b.rearrange("l (c p) -> (l c) p", p=P)),
                         ("ln_g", cf_ln_g.rearrange("l (c p) -> (l c) p", p=P)),
                         ("ln_b", cf_ln_b.rearrange("l (c p) -> (l c) p", p=P)),
                         ("pw2_b", cf_b_pw2.rearrange("l (c p) -> (l c) p", p=P))):
            prow[name] = n
            loads.append((n, ap))
            n += ap.shape[0]
        assert n == NPAR <= P

        def par(name, i):
            return params[:, prow[name] + i:prow[name] + i + 1]

        keys_dram = peer_sub_keys.rearrange("l s n c -> n (l s) c")
        u_rows = peer_u.rearrange("l e d -> (l e) d")
        v_rows = peer_v.rearrange("l e d -> (l e) d")

        s_par = sem("s_par")
        s_x = sem("s_x")
        s_keys = sem("s_keys")
        s_cw = sem("s_cw")
        s_w = [sem(f"s_w{b}") for b in range(NB)]
        s_const = sem("s_const")
        s_pdve = sem("s_pdve")
        s_tp = sem("s_tp")
        s_tpe = sem("s_tpe")
        s_sq = sem("s_sq")
        s_ss = sem("s_ss")
        s_rms = sem("s_rms")
        s_y = sem("s_y")
        s_proj = sem("s_proj")
        s_bank = [sem(f"s_bank{b}") for b in range(2)]
        s_vt = sem("s_vt")
        s_vte = sem("s_vte")
        s_z = sem("s_z")
        s_ze = sem("s_ze")
        s_zz = sem("s_zz")
        s_abs = sem("s_abs")
        s_e0 = sem("s_e0")
        s_ln = sem("s_ln")
        s_spl = sem("s_spl")
        s_spm = sem("s_spm")
        s_suf = sem("s_suf")
        s_lw = sem("s_lw")
        s_ew = sem("s_ew")
        s_wm = sem("s_wm")
        s_av = sem("s_av")
        s_ave = sem("s_ave")
        s_b = sem("s_b")
        s_pad = sem("s_pad")
        s_res = sem("s_res")
        s_gz = sem("s_gz")
        s_cv = sem("s_cv")
        s_mu = sem("s_mu")
        s_xc = sem("s_xc")
        s_xn = sem("s_xn")
        s_sz = sem("s_sz")
        s_chain = sem("s_chain")
        s_qg = sem("s_qg")
        s_yg = sem("s_yg")
        s_sc = sem("s_sc")
        s_yr = sem("s_yr")
        s_top = sem("s_top")
        s_exp = sem("s_exp")
        s_idx = sem("s_idx")
        s_idv = sem("s_idv")
        s_u = [sem(f"s_u{k}") for k in range(TOPK)]
        s_v = [sem(f"s_v{k}") for k in range(TOPK)]
        s_dot = sem("s_dot")
        s_gel = sem("s_gel")
        s_m = sem("s_m")
        s_vm = sem("s_vm")
        s_oe = sem("s_oe")
        s_ot = sem("s_ot")
        s_ha = sem("s_ha")
        s_rdy = sem("s_rdy")
        s_ft = sem("s_ft")
        s_fe = sem("s_fe")
        s_out = sem("s_out")
        s_turn = {e: sem("s_turn_" + e) for e in ("pool", "dve", "act", "pe")}

        def hold(eng, name, s, value):
            eng.wait_ge(s, value)
            if not isinstance(value, int):
                eng.sem_inc(s_turn[name], 1)

        w_in, w_out = ab_w_in[0], ab_w_out[0]
        w_pw1, w_pw2 = cf_w_pw1[0], cf_w_pw2[0]
        w_q = [peer_w_q[i] for i in range(2)]
        SEQW = [("in", w_in, 24), ("out", w_out, 8), ("q0", w_q[0], 16)]
        for i in range(len(BLOCKS)):
            SEQW += [("pw1%d" % i, w_pw1, 16), ("pw2%d" % i, w_pw2, 8), ("q1%d" % i, w_q[1], 16)]
        first = {}
        at = 0
        for name, _, k in SEQW:
            first[name] = at
            at += k
        sums_before = {"in": 1, "out": 1, "q0": 2}
        for i in range(len(BLOCKS)):
            sums_before.update({"pw1%d" % i: 3 + 4 * i, "pw2%d" % i: 5 + 4 * i, "q1%d" % i: 6 + 4 * i})

        def turn(name, k):
            return first[name] + k + 2 * sums_before[name]

        G0, G1 = L // GT, SEQ // GT
        N = G0 + G1
        GB = BLOCKS[1][0] // GT
        SIDE = 8
        assert GB + SIDE == G0 and G0 + SIDE < N - 1

        def token(n, layer):
            return n * GT - layer * (G0 - 1) * GT

        def layer_of(n):
            return int(n >= G0)

        def step(n):
            if isinstance(n, int) and GB <= n < GB + 2 * SIDE:
                return (n - GB) // SIDE, (n - GB) % SIDE
            return 0, None

        def pipeline(eng, body):
            body(0, 0, False, True)
            with eng.Fori(1, GB) as n:
                body(n, 0, True, True)
            for n in range(GB, GB + 2 * SIDE):
                body(n, layer_of(n), True, True)
            with eng.Fori(GB + 2 * SIDE, N - 1) as n:
                body(n, 1, True, True)
            body(N - 1, 1, True, False)

        block = ctx.enter_context(nc.Block())

        @block.sync
        def _(sp):
            for r, ap in loads:
                sp.dma_start(pin[r:r + ap.shape[0], :], ap).then_inc(s_par, 16)
            for i in range(TILES):
                sp.dma_start(xin[:, i, :], x[0, i * P:(i + 1) * P, :]).then_inc(s_x, 16)
            sp.dma_start(min_[0:META, :], meta_tokens).then_inc(s_x, 16)
            sp.dma_start(kin, keys_dram).then_inc(s_keys, 16)
            sp.dma_start(cin[0:CK, :], cf_conv_w[0]).then_inc(s_cw, 16)

            def chunk(w, b, col):
                return sp.dma_start(wring[:, b, :, :], w.rearrange("(c p) n -> p c n", p=P)[:, :, col]).then_inc(s_w[b], 16)

            for name, w, k in SEQW:
                if first[name] == 0:
                    for b in range(NB):
                        chunk(w, b, bass.ts(b, P))
                    lo = 1
                else:
                    lo = 0
                with sp.Fori(lo, k // NB) if k // NB - lo > 1 else ExitStack() as r:
                    if k // NB - lo <= 1:
                        r = lo
                    for b in range(NB):
                        sp.wait_ge(s_proj, first[name] + r * NB + b - NB + 1)
                        if name[:3] == "pw1":
                            col = bass.ds(r * (NB // 2 * P) + (b % 2) * D + b // 2 * P, P)
                        else:
                            col = bass.ds(r * (NB * P) + b * P, P)
                        chunk(w, b, col)
            sp.wait_ge(s_fe, TILES * 2)
            sp.dma_start(out[0].rearrange("(i p) d -> p i d", p=P), outs).then_inc(s_out, 16)
            sp.wait_ge(s_out, 16)

        @block.gpsimd
        def _(pool):
            nc.gpsimd.memset(ident[:, :], 0.0).then_inc(s_const, 1)
            nc.gpsimd.memset(ones[:, :], 1.0).then_inc(s_const, 1)
            nc.gpsimd.memset(epsc[:, :], EPS).then_inc(s_const, 1)
            nc.gpsimd.iota(iota16[:, :], [[1, TOPK]], base=0, channel_multiplier=0,
                           allow_small_or_imprecise_dtypes=True).then_inc(s_const, 1)
            pool.wait_ge(s_const, 4)
            nc.gpsimd.affine_select(out=ident[:, :], in_=ident[:, :], compare_op=ALU.not_equal, fill=1.0, base=0,
                                    pattern=[[-1, P]], channel_multiplier=1).then_inc(s_const, 1)
            nc.gpsimd.affine_select(out=tri[:, :], in_=ones[:, :], compare_op=ALU.is_ge, fill=0.0, base=0,
                                    pattern=[[-1, P]], channel_multiplier=1).then_inc(s_const, 1)
            nc.gpsimd.memset(gz[:, :, 0:CK - 1], 0.0).then_inc(s_pad, 1)
            pool.wait_ge(s_tpe, 9)
            nc.gpsimd.memset(cx[:, :, 0:KC - 1], 0.0).then_inc(s_pad, 1)
            nc.gpsimd.memset(Z[:, :, KO[2]:ZW], 0.0).then_inc(s_zz, 1)

            def mask(t, half, done):
                for (k0, kn), ko in zip(KT, KO):
                    v = t[0:kn, half * (AH // 2):(half + 1) * (AH // 2), ko:ko + kn]
                    nc.gpsimd.affine_select(out=v, in_=v, compare_op=ALU.is_gt, fill=0.0, base=0,
                                            pattern=[[0, AH // 2], [1, kn]], channel_multiplier=-1).then_inc(done, 1)

            for half in range(2):
                pool.wait_ge(s_spl, half + 1)
                mask(S, half, s_spm)
            for half in range(2):
                pool.wait_ge(s_ew, half + 1)
                mask(A, half, s_wm)

            def gathers(n, layer, before, after):
                hold(pool, "pool", s_idx, n + 1)
                for k in range(TOPK):
                    hold(pool, "pool", s_dot, n * TOPK + k + 1)
                    pool.indirect_dma_start(out=rowsU[:, k % NU, :], out_offset=None, in_=u_rows,
                                            in_offset=bass.IndirectOffsetOnAxis(ap=expU[:, k:k + 1], axis=0)
                                            ).then_inc(s_u[k % NU], 16)
                hold(pool, "pool", s_vm, n * TOPK + 1)
                nc.gpsimd.tensor_copy(expV[:, :], expU[:, :]).then_inc(s_idv, 1)
                hold(pool, "pool", s_idv, n + 2)
                for k in range(TOPK):
                    pool.indirect_dma_start(out=rowsV[:, k, :], out_offset=None, in_=v_rows,
                                            in_offset=bass.IndirectOffsetOnAxis(ap=expV[:, k:k + 1], axis=0)
                                            ).then_inc(s_v[k], 16)

            pool.sem_inc(s_idv, 1)
            pool.wait_ge(s_y, 2)
            with pool.Fori(0, N) as n:
                gathers(n, 0, True, True)

        @block.scalar
        def _(act):
            act.sem_inc(s_bank[0], 1)
            act.sem_inc(s_bank[1], 1)
            act.sem_inc(s_ha, 1)
            act.sem_inc(s_ot, 1)
            act.sem_inc(s_dot, NU)
            act.sem_inc(s_vm, 1)
            act.wait_ge(s_tp, 1)
            act.copy(params[:, :], ps[:, 0, 0:NPAR]).then_inc(s_tpe, 1)
            for i in range(TILES):
                for q in range(2):
                    act.wait_ge(s_tp, 2 + 2 * i + q)
                    act.copy(hT[:, 4 * q:4 * q + 4, META + i * P:META + (i + 1) * P],
                             ps[:, 1 + 2 * i + q, :].rearrange("p (c t) -> p c t", t=P)).then_inc(s_tpe, 1)
            act.wait_ge(s_tp, 6)
            act.copy(hT[:, :, 0:META], ps[:, 5, 0:C * META].rearrange("p (c t) -> p c t", t=META)).then_inc(s_tpe, 1)
            act.wait_ge(s_tp, 7)
            act.copy(keysT[:, :, :], ps[:, 6, :].rearrange("p (s k) -> p s k", k=NK)).then_inc(s_tpe, 1)
            act.wait_ge(s_tp, 8)
            act.copy(convT[:, :, :], ps[:, 7, 0:C * CK].rearrange("p (c k) -> p c k", k=CK)).then_inc(s_tpe, 1)
            act.wait_ge(s_tpe, 8)
            act.sem_inc(s_tpe, 1)

            def free_both(s, value):
                act.wait_ge(s, value)
                act.sem_inc(s_bank[0], 1)
                act.sem_inc(s_bank[1], 1)

            def root(m, w):
                act.wait_ge(s_ss, m)
                act.activation(rstd[:, 0:w], ps[:, 0, 0:w], ACT.Sqrt, bias=epsc[:, :], scale=1.0 / D).then_inc(s_rms, 1)
                free_both(s_rms, m)

            def evacuate(name, count, dst):
                n0 = first[name]
                with act.Fori(0, count // NB) as r:
                    for b in range(NB):
                        hold(act, "act", s_proj, n0 + r * NB + b + 1)
                        act.copy(dst(r, b), ps[:, b % 2, 0:L]).then_inc(s_bank[b % 2], 1)

            act.activation(sq[:, :, :], hT[:, :, :], ACT.Square).then_inc(s_sq, 1)
            root(1, L)
            evacuate("in", 24, lambda r, b: proj[:, bass.ds(r * NB + b, 1), :].rearrange("p a t -> p (a t)"))
            act.wait_ge(s_zz, 1)
            for h in range(AH):
                act.wait_ge(s_z, h + 1)
                b = 2 + h % 6
                act.activation(Z[:, h, 0:KO[2]], ps[:, b, 0:KO[2]], ACT.Copy, scale=DH ** -0.5).then_inc(s_ze, 1)
                act.activation(Z[0:KT[2][1], h, KO[2]:ZW], ps[0:KT[2][1], b, KO[2]:ZW], ACT.Copy,
                               scale=DH ** -0.5).then_inc(s_ze, 1)
            HH = AH // 2
            for half in range(2):
                a = A[:, half * HH:(half + 1) * HH, :]
                act.wait_ge(s_ze, (half + 1) * AH)
                act.activation(a, Z[:, half * HH:(half + 1) * HH, :], ACT.Abs).then_inc(s_abs, 1)
                act.wait_ge(s_abs, half + 1)
                act.activation(a, a, ACT.Exp, scale=-1.0).then_inc(s_e0, 1)
                act.wait_ge(s_e0, half + 1)
                act.activation(a, a, ACT.Ln, bias=1.0).then_inc(s_ln, 1)
            for half in range(2):
                act.wait_ge(s_lw, (half + 1) * AH)
                act.activation(A[:, half * HH:(half + 1) * HH, :], Z[:, half * HH:(half + 1) * HH, :],
                               ACT.Exp).then_inc(s_ew, 1)
            for c in range(AC):
                act.wait_ge(s_av, 2 * c + 2)
                act.copy(mixT[:, c, :], ps[:, 2 + c, 0:L]).then_inc(s_ave, 1)

            act.wait_ge(s_res, C)
            act.activation(sq[:, :, :], hT[:, :, :], ACT.Square).then_inc(s_sq, 1)
            root(2, L)
            with act.Fori(0, 16 // NB) as r:
                for b in range(NB):
                    hold(act, "act", s_proj, first["q0"] + r * NB + b + 1)
                    act.copy(qT[:, bass.ds(r * (NB // 2) + b // 2, 1), b % 2, :].rearrange("p a t -> p (a t)"),
                             ps[:, b % 2, 0:L]).then_inc(s_bank[b % 2], 1)

            def prepare(n, layer):
                if isinstance(n, int) and n in (0, G0):
                    q = ("q0", 16) if n == 0 else ("q10", 16)
                    act.wait_ge(s_bank[0], 1 + turn(*q) // 2)
                    act.wait_ge(s_bank[1], 1 + turn(*q) // 2)
                if isinstance(n, int) and n == G0 + SIDE:
                    act.wait_ge(s_bank[0], 1 + turn("q11", 16) // 2)
                    act.wait_ge(s_bank[1], 1 + turn("q11", 16) // 2)
                if not (isinstance(n, int) and n == 0):
                    hold(act, "act", s_sc, n)
                act.copy(qg[:, :, :, :], qT[:, :, :, bass.ds(token(n, layer), GT)].rearrange("p h s t -> p s h t")
                         ).then_inc(s_qg, 1)
                if not (isinstance(n, int) and n == 0):
                    hold(act, "act", s_yr, n)
                for h in range(H):
                    act.copy(yg[:, :, h, :], yT[:, :, bass.ds(token(n, layer), GT)]).then_inc(s_yg, 1)

            def exps(n):
                hold(act, "act", s_top, n + 1)
                act.activation(gexp[:, :], topv[:, :], ACT.Exp, bias=negm[:, :], accum_out=gsum[:, :]
                               ).then_inc(s_exp, 1)

            def early(n):
                w, j = step(n)
                if j == 1:
                    root(3 + 3 * w, BLOCKS[w][1])
                if j == 6:
                    root(5 + 3 * w, P)

            def beside(n):
                w, j = step(n)
                c0, wi, o0 = BLOCKS[w]
                if j in (1, 2):
                    if j == 2 or w:
                        act.wait_ge(s_gz, 2 * w + j - 1)
                    for c in range(C // 2):
                        act.wait_ge(s_proj, first["pw1%d" % w] + (j - 1) * C + 2 * c + 1)
                        act.activation(ga[:, c, 0:wi], ps[:, 0, 0:wi], ACT.Identity,
                                       bias=par("pw1_b", (j - 1) * (C // 2) + c)).then_inc(s_bank[0], 1)
                        act.wait_ge(s_proj, first["pw1%d" % w] + (j - 1) * C + 2 * c + 2)
                        act.activation(sg[:, c, 0:wi], ps[:, 1, 0:wi], ACT.Sigmoid,
                                       bias=par("pw1_b", C + (j - 1) * (C // 2) + c)).then_inc(s_bank[1], 1)
                if j == 4:
                    act.wait_ge(s_xc, w + 1)
                    act.activation(sqb[:, :, 0:P], cv[:, :, :], ACT.Square).then_inc(s_sq, 1)
                    root(4 + 3 * w, P)
                if j == 5:
                    for c in range(C):
                        act.wait_ge(s_proj, first["pw2%d" % w] + c + 1)
                        act.activation(sqb[:, c, 0:P], ps[:, c % 2, 0:P], ACT.Identity, bias=par("pw2_b", c)
                                       ).then_inc(s_bank[c % 2], 1)
                if j in (6, 7):
                    for k in range(C):
                        kk = (j - 6) * C + k
                        act.wait_ge(s_proj, first["q1%d" % w] + kk + 1)
                        act.copy(qT[:, kk // 2, kk % 2, o0:o0 + P], ps[:, kk % 2, 0:P]).then_inc(s_bank[kk % 2], 1)

            def late(n):
                w, j = step(n)
                c0, wi, o0 = BLOCKS[w]
                if j == 0:
                    act.wait_ge(s_ha, 1 + n)
                    act.activation(sqb[:, :, 0:wi], hT[:, :, c0:c0 + wi], ACT.Square).then_inc(s_sq, 1)
                if j == 4:
                    act.wait_ge(s_xn, w + 1)
                    for c in range(C):
                        act.activation(cv[:, c, :], cv[:, c, :], ACT.Silu, bias=par("ln_b", c), scale=par("ln_g", c)
                                       ).then_inc(s_sz, 1)
                if j == 5:
                    act.wait_ge(s_res, C + 1 + w)
                    act.activation(sqb[:, :, 0:P], hT[:, :, o0:o0 + P], ACT.Square).then_inc(s_sq, 1)

            def evacuate_output(n):
                hold(act, "act", s_vm, 1 + n * TOPK)
                hold(act, "act", s_ot, n)
                act.copy(osb[:, :], po[0:GT, :, :].rearrange("p a b -> p (a b)")).then_inc(s_oe, 1)

            def body(n, layer, before, after):
                if before:
                    evacuate_output(n)
                early(n)
                last_step = step(n)[1] == SIDE - 1
                nl = layer_of(n + 1) if isinstance(n, int) else layer
                if after and not last_step:
                    prepare(n + 1, nl)
                beside(n)
                if after and last_step:
                    prepare(n + 1, nl)
                hold(act, "act", s_dot, NU + (n + 1) * TOPK)
                act.activation(gel[:, :], dots[:, :], ACT.Gelu).then_inc(s_gel, 1)
                if after:
                    exps(n + 1)
                late(n)

            prepare(0, 0)
            exps(0)
            pipeline(act, body)
            evacuate_output(N)

            act.wait_ge(s_ha, 1 + N)
            act.activation(sq[:, :, 0:SEQ], hT[:, :, META:L], ACT.Square).then_inc(s_sq, 1)
            root(9, SEQ)
            for i in range(TILES):
                for q in range(2):
                    act.wait_ge(s_ft, 2 * i + q + 1)
                    act.copy(outs[:, i, 512 * q:512 * (q + 1)], ps[:, 2 * i + q, :]).then_inc(s_fe, 1)

        @block.tensor
        def _(pe):
            pe.wait_ge(s_const, 6)
            pe.wait_ge(s_par, 16 * len(loads))
            pe.transpose(ps[:, 0, 0:NPAR], pin[0:NPAR, :], ident[0:NPAR, 0:NPAR]).then_inc(s_tp, 1)
            pe.wait_ge(s_x, 16 * (TILES + 1))
            for i in range(TILES):
                for q in range(2):
                    for c in range(4):
                        last = pe.transpose(ps[:, 1 + 2 * i + q, c * P:(c + 1) * P],
                                            xin[:, i, (4 * q + c) * P:(4 * q + c + 1) * P], ident[:, :])
                    last.then_inc(s_tp, 1)
            for c in range(C):
                last = pe.transpose(ps[:, 5, c * META:(c + 1) * META], min_[0:META, c * P:(c + 1) * P],
                                    ident[0:META, 0:META])
            last.then_inc(s_tp, 1)
            pe.wait_ge(s_keys, 16)
            for s in range(4):
                last = pe.transpose(ps[:, 6, s * NK:(s + 1) * NK], kin[:, s, :], ident[:, :])
            last.then_inc(s_tp, 1)
            pe.wait_ge(s_cw, 16)
            for c in range(C):
                last = pe.transpose(ps[:, 7, c * CK:(c + 1) * CK], cin[0:CK, c * P:(c + 1) * P], ident[0:CK, 0:CK])
            last.then_inc(s_tp, 1)
            pe.wait_ge(s_tpe, 9)

            def sums(src, w, s, ready, name):
                pe.wait_ge(*ready)
                t = turn(name, 0) // 2 - (2 if s is s_mu else 1)
                pe.wait_ge(s_bank[0], t + 1)
                for c in range(C):
                    last = pe.matmul(ps[:, 0, 0:w], ones[:, :], src[:, c, 0:w], start=(c == 0), stop=(c == C - 1))
                last.then_inc(s, 1)

            def chunk(name, k, b, rhs, w, r=0):
                pe.wait_ge(s_w[b], (r + (first[name] + k) // NB) * 16 + 16)
                pe.wait_ge(s_bank[b % 2], r * (NB // 2) + turn(name, k) // 2 + 1)
                for c in range(C):
                    last = pe.matmul(ps[:, b % 2, 0:w], wring[:, b, c, :], rhs(c), start=(c == 0), stop=(c == C - 1))
                last.then_inc(s_proj, 1)

            def project(name, count, rhs, w):
                with pe.Fori(0, count // NB) as r:
                    for b in range(NB):
                        chunk(name, b, b, rhs, w, r)

            sums(sq, L, s_ss, (s_sq, 1), "in")
            pe.wait_ge(s_y, 1)
            project("in", 24, lambda c: yT[:, c, :], L)

            pe.wait_ge(s_bank[0], 1 + turn("in", 24) // 2)
            pe.wait_ge(s_bank[1], 1 + turn("in", 24) // 2)
            for t, (k0, kn) in enumerate(KT):
                for c in range(AC):
                    last = pe.transpose(ps[0:kn, 5 + t, c * P:(c + 1) * P], proj[:, 2 * AC + c, k0:k0 + kn], ident[:, :])
                last.then_inc(s_vt, 1)
            for h in range(AH):
                c, q0 = h // 2, DH * (h % 2)
                if h == 3:
                    pe.wait_ge(s_vte, 3)
                if h >= 6:
                    pe.wait_ge(s_ze, 2 * (h - 5))
                for (k0, kn), ko, kw in zip(KT, KO, KW):
                    last = pe.matmul(ps[0:kn, 2 + h % 6, ko:ko + kw], proj[q0:q0 + DH, AC + c, k0:k0 + kn],
                                     proj[q0:q0 + DH, c, k0:L], start=True, stop=True)
                last.then_inc(s_z, 1)
            for h in range(AH):
                if h == 0:
                    pe.wait_ge(s_ze, 2 * AH)
                if h % (AH // 2) == 0:
                    pe.wait_ge(s_spm, 3 * (h // (AH // 2) + 1))
                b = 2 + h % 6
                if h >= 6:
                    pe.wait_ge(s_lw, 2 * (h - 5))
                for i, ((k0, kn), ko, kw) in enumerate(zip(KT, KO, KW)):
                    for j in range(i, 3):
                        (j0, jn), jo, jw = KT[j], KO[j], KW[j]
                        d = j0 - k0
                        last = pe.matmul(ps[0:kn, b, ko + d:ko + kw], (tri if i == j else ones)[0:jn, 0:kn],
                                         S[0:jn, h, jo:jo + jw], start=(j == i), stop=(j == 2))
                last.then_inc(s_suf, 1)
            for h in range(AH):
                if h == 0:
                    pe.wait_ge(s_lw, 2 * AH)
                if h % (AH // 2) == 0:
                    pe.wait_ge(s_wm, 3 * (h // (AH // 2) + 1))
                c, q0 = h // 2, DH * (h % 2)
                for j in range(3):
                    (j0, jn), jo, jw = KT[j], KO[j], KW[j]
                    last = pe.matmul(ps[q0:q0 + DH, 2 + c, j0:L], vtok[0:jn, j, h * DH:(h + 1) * DH],
                                     A[0:jn, h, jo:jo + jw], start=(j == 0), stop=(j == 2))
                last.then_inc(s_av, 1)
            pe.wait_ge(s_ave, AC)
            pe.wait_ge(s_b, AC)
            project("out", 8, lambda c: mixT[:, c, :], L)

            sums(sq, L, s_ss, (s_sq, 2), "q0")
            pe.wait_ge(s_y, 2)
            project("q0", 16, lambda c: yT[:, c, :], L)

            def scores(n, layer):
                hold(pe, "pe", s_qg, n + 1)
                if not isinstance(n, int) or n:
                    hold(pe, "pe", s_top, n)
                for s in range(2):
                    last = pe.matmul(psc[:, s * NK:(s + 1) * NK], qg[:, s, :, :].rearrange("p h t -> p (h t)"),
                                     keysT[:, 2 * layer + s, :], start=True, stop=True)
                last.then_inc(s_sc, 1)

            def rows(n):
                hold(pe, "pe", s_yg, H * (n + 1))
                hold(pe, "pe", s_dot, NU + n * TOPK)
                for c in range(C):
                    last = pe.transpose(yrep[:, c * P:(c + 1) * P], yg[:, c, :, :].rearrange("p h t -> p (h t)"),
                                        ident[:, :])
                last.then_inc(s_yr, 1)

            def values(n):
                hold(pe, "pe", s_m, n + 1)
                if not isinstance(n, int) or n:
                    hold(pe, "pe", s_oe, n)
                for k in range(TOPK):
                    hold(pe, "pe", s_v[k], 16 * (n + 1))
                    for q in range(2):
                        last = pe.matmul(po[0:GT, q, :], mix[:, k, :], rowsV[:, k, 512 * q:512 * (q + 1)],
                                         start=(k == 0), stop=(k == TOPK - 1))
                    last.then_inc(s_vm, 1)

            def back(n):
                hold(pe, "pe", s_oe, n)
                hold(pe, "pe", s_ha, n)
                for c in range(C):
                    last = pe.transpose(pt[:, c, :], osb[:, c * P:(c + 1) * P], ident[0:GT, 0:GT])
                last.then_inc(s_ot, 1)

            def early(n):
                w, j = step(n)
                c0, wi, o0 = BLOCKS[w]
                if j == 1:
                    sums(sqb, wi, s_ss, (s_sq, 3 + 3 * w), "pw1%d" % w)
                if j == 4:
                    sums(cv, P, s_mu, (s_cv, C * (w + 1)), "pw2%d" % w)
                if j == 6:
                    sums(sqb, P, s_ss, (s_sq, 5 + 3 * w), "q1%d" % w)

            def beside(n):
                w, j = step(n)
                c0, wi, o0 = BLOCKS[w]
                if j in (1, 2):
                    pe.wait_ge(s_y, 3 + 2 * w)
                    for k in range((j - 1) * C, j * C):
                        chunk("pw1%d" % w, k, k % NB, lambda c: yT[:, c, c0:c0 + wi], wi)
                if j == 4:
                    sums(sqb, P, s_ss, (s_sq, 4 + 3 * w), "pw2%d" % w)
                if j == 5:
                    pe.wait_ge(s_sz, C * (w + 1))
                    for k in range(C):
                        chunk("pw2%d" % w, k, k % NB, lambda c: cv[:, c, :], P)
                if j in (6, 7):
                    pe.wait_ge(s_y, 4 + 2 * w)
                    for k in range((j - 6) * C, (j - 5) * C):
                        chunk("q1%d" % w, k, k % NB, lambda c: yT[:, c, o0:o0 + P], P)

            def body(n, layer, before, after):
                early(n)
                if before:
                    back(n)
                last_step = step(n)[1] == SIDE - 1
                nl = layer_of(n + 1) if isinstance(n, int) else layer
                if after and not last_step:
                    scores(n + 1, nl)
                beside(n)
                if after and last_step:
                    scores(n + 1, nl)
                if after:
                    rows(n + 1)
                values(n)

            scores(0, 0)
            rows(0)
            pipeline(pe, body)
            back(N)

            pe.wait_ge(s_sq, 9)
            pe.wait_ge(s_bank[0], 1 + turn("q11", 16) // 2)
            for c in range(C):
                last = pe.matmul(ps[:, 0, 0:SEQ], ones[:, :], sq[:, c, 0:SEQ], start=(c == 0), stop=(c == C - 1))
            last.then_inc(s_ss, 1)
            pe.wait_ge(s_rdy, 1)
            for i in range(TILES):
                for q in range(2):
                    for c in range(4):
                        last = pe.transpose(ps[:, 2 * i + q, c * P:(c + 1) * P], yF[:, 4 * q + c, i * P:(i + 1) * P],
                                            ident[:, :])
                    last.then_inc(s_ft, 1)

        @block.vector
        def _(dve):
            chain = [0]

            def link(ins):
                chain[0] += 1
                ins.then_inc(s_chain, 1)
                dve.wait_ge(s_chain, chain[0])

            def norm(m, dst, src, gains, w, done):
                dve.wait_ge(s_rms, m)
                link(nc.vector.reciprocal(rstd[:, 0:w], rstd[:, 0:w]))
                for c in range(C):
                    last = nc.vector.scalar_tensor_tensor(out=dst[:, c, :], in0=src[:, c, :], scalar=par(gains[0], gains[1] + c),
                                                          in1=rstd[:, 0:w], op0=ALU.mult, op1=ALU.mult)
                last.then_inc(done, 1)

            dve.wait_ge(s_const, 6)
            nc.vector.tensor_reduce(out=sel[:, :], in_=ident[:, :].rearrange("p (h t) -> p t h", t=GT), axis=AX,
                                    op=ALU.add).then_inc(s_pdve, 1)
            dve.wait_ge(s_tpe, 9)
            norm(1, yT[:, :, :], hT[:, :, :], ("mix_g", 0), L, s_y)

            for t, (k0, kn) in enumerate(KT):
                dve.wait_ge(s_vt, t + 1)
                nc.vector.tensor_copy(vtok[0:kn, t, :], ps[0:kn, 5 + t, :]).then_inc(s_vte, 1)
            HH = AH // 2
            dve.wait_ge(s_pad, 2)
            link(nc.vector.tensor_tensor(cx[:, :, KC - 1:], proj[:, 4 * AC:5 * AC, :], proj[:, 5 * AC:6 * AC, :], ALU.mult))
            for c in range(AC):
                nc.vector.tensor_scalar(ct[:, c, :], cx[:, c, 0:L], par("ab_w", c), None, ALU.mult).then_inc(s_chain, 1)
                chain[0] += 1
            for k in range(1, KC):
                for c in range(AC):
                    dve.wait_ge(s_chain, chain[0] - AC + 1)
                    nc.vector.scalar_tensor_tensor(out=ct[:, c, :], in0=cx[:, c, k:k + L], scalar=par("ab_w", k * AC + c),
                                                   in1=ct[:, c, :], op0=ALU.mult, op1=ALU.add).then_inc(s_chain, 1)
                    chain[0] += 1
            for half in range(2):
                sl = slice(half * HH, (half + 1) * HH)
                dve.wait_ge(s_ln, half + 1)
                nc.vector.scalar_tensor_tensor(out=S[:, sl, :].rearrange("p a b -> p (a b)"),
                                               in0=Z[:, sl, :].rearrange("p a b -> p (a b)"), scalar=0.0,
                                               in1=A[:, sl, :].rearrange("p a b -> p (a b)"), op0=ALU.max,
                                               op1=ALU.add).then_inc(s_spl, 1)
            for c in range(AC):
                dve.wait_ge(s_chain, chain[0] - AC + 1 + c)
                nc.vector.tensor_tensor(mixT[:, AC + c, :], proj[:, 3 * AC + c, :], ct[:, c, :], ALU.mult).then_inc(s_b, 1)
            for h in range(AH):
                dve.wait_ge(s_suf, h + 1)
                b = 2 + h % 6
                nc.vector.tensor_tensor(Z[:, h, 0:KO[2]], Z[:, h, 0:KO[2]], ps[:, b, 0:KO[2]], ALU.subtract).then_inc(s_lw, 1)
                z2 = Z[0:KT[2][1], h, KO[2]:ZW]
                nc.vector.tensor_tensor(z2, z2, ps[0:KT[2][1], b, KO[2]:ZW], ALU.subtract).then_inc(s_lw, 1)
            for c in range(C):
                dve.wait_ge(s_proj, first["out"] + c + 1)
                nc.vector.tensor_tensor(hT[:, c, :], hT[:, c, :], ps[:, c % 2, 0:L], ALU.add).then_inc(s_res, 1)
                dve.wait_ge(s_res, c + 1)
                dve.sem_inc(s_bank[c % 2], 1)

            def route(n, layer):
                hold(dve, "dve", s_sc, n + 1)
                sc = [psc[:, s * NK:(s + 1) * NK] for s in range(2)]
                for s in range(2):
                    nc.vector.max(val[:, s, 0:8], sc[s])
                dve.drain()
                for s in range(2):
                    nc.vector.max_index(idx[:, s, 0:8], val[:, s, 0:8], sc[s])
                    nc.vector.match_replace(rest[:, s, :], val[:, s, 0:8], sc[s], LOW)
                dve.drain()
                for s in range(2):
                    nc.vector.max(val[:, s, 8:16], rest[:, s, :])
                dve.drain()
                for s in range(2):
                    nc.vector.max_index(idx[:, s, 8:16], val[:, s, 8:16], rest[:, s, :])
                nc.vector.tensor_tensor(cand[:, :, :], val[:, 0, :].unsqueeze(2).to_broadcast([P, TOPK, TOPK]),
                                        val[:, 1, :].unsqueeze(1).to_broadcast([P, TOPK, TOPK]), ALU.add)
                dve.drain()
                c1 = cand[:, :, :].rearrange("p a b -> p (a b)")
                c2 = cand2[:, :, :].rearrange("p a b -> p (a b)")
                nc.vector.max(topv[:, 0:8], c1)
                nc.vector.tensor_scalar(idxf[:, 0, :], idx[:, 0, :], float(NK), None, ALU.mult)
                nc.vector.tensor_scalar(idxf[:, 1, :], idx[:, 1, :], float(layer * NE), None, ALU.add)
                dve.drain()
                nc.vector.max_index(topp[:, 0:8], topv[:, 0:8], c1)
                nc.vector.match_replace(c2, topv[:, 0:8], c1, LOW)
                nc.vector.tensor_scalar(negm[:, :], topv[:, 0:1], -1.0, None, ALU.mult)
                dve.drain()
                nc.vector.max(topv[:, 8:16], c2).then_inc(s_top, 1)
                dve.drain()
                nc.vector.max_index(topp[:, 8:16], topv[:, 8:16], c2)
                dve.drain()
                nc.vector.tensor_scalar(posu[:, 0, :], topp[:, :], 4, None, ALU.logical_shift_right)
                nc.vector.tensor_scalar(posu[:, 1, :], topp[:, :], 15, None, ALU.bitwise_and)
                dve.drain()
                nc.vector.tensor_copy(posf[:, :, :], posu[:, :, :])
                dve.drain()
                for s in range(2):
                    nc.vector.tensor_tensor(hot[:, s, :, :], posf[:, s, :].unsqueeze(2).to_broadcast([P, TOPK, TOPK]),
                                            iota16[:, :].unsqueeze(1).to_broadcast([P, TOPK, TOPK]), ALU.is_equal)
                dve.drain()
                for s in range(2):
                    nc.vector.tensor_tensor(hot[:, s, :, :], hot[:, s, :, :],
                                            idxf[:, s, :].unsqueeze(1).to_broadcast([P, TOPK, TOPK]), ALU.mult)
                dve.drain()
                nc.vector.tensor_reduce(out=picked[:, :, :], in_=hot[:, :, :, :], axis=AX, op=ALU.add)
                dve.drain()
                hold(dve, "dve", s_idv, n + 1)
                nc.vector.tensor_tensor(expU[:, :], picked[:, 0, :], picked[:, 1, :], ALU.add).then_inc(s_idx, 1)

            def mid(n):
                w, j = step(n)
                c0, wi, o0 = BLOCKS[w]
                if j == 1:
                    norm(3 + 3 * w, yT[:, :, c0:c0 + wi], hT[:, :, c0:c0 + wi], ("mix_g", C), wi, s_y)
                if j == 4:
                    dve.wait_ge(s_mu, w + 1)
                    link(nc.vector.tensor_scalar(mu[:, :], ps[:, 0, 0:P], 1.0 / D, None, ALU.mult))
                    dve.sem_inc(s_bank[0], 1)
                    dve.sem_inc(s_bank[1], 1)
                    nc.vector.tensor_tensor(cv[:, :, :], cv[:, :, :], mu[:, :].unsqueeze(1).to_broadcast([P, C, P]),
                                            ALU.subtract).then_inc(s_xc, 1)
                if j == 6:
                    norm(5 + 3 * w, yT[:, :, o0:o0 + P], hT[:, :, o0:o0 + P], ("ffn_g", C), P, s_y)

            def late(n):
                w, j = step(n)
                c0, wi, o0 = BLOCKS[w]
                if j in (1, 2):
                    for b in range(2):
                        dve.wait_ge(s_bank[b], 1 + turn("pw1%d" % w, j * C) // 2)
                    if j == 1:
                        dve.wait_ge(s_pad, 1)
                    half = slice((j - 1) * (C // 2), j * (C // 2))
                    nc.vector.tensor_tensor(gz[:, half, CK - 1 + c0:CK - 1 + c0 + wi], ga[:, :, 0:wi], sg[:, :, 0:wi],
                                            ALU.mult).then_inc(s_gz, 1)
                    dve.wait_ge(s_gz, 2 * w + j)
                chunks = {1: (0, 1), 2: (2, 3, 4), 3: (5, 6, 7)}.get(j, ())
                for k in range(CK if chunks else 0):
                    for c in chunks:
                        tap, src = convT[:, c, k:k + 1], gz[:, c, o0 + k:o0 + k + P]
                        if k == 0:
                            ins = nc.vector.tensor_scalar(cv[:, c, :], src, tap, par("cv_b", c), ALU.mult, ALU.add)
                        else:
                            dve.wait_ge(s_chain, chain[0] - len(chunks) + 1)
                            ins = nc.vector.scalar_tensor_tensor(out=cv[:, c, :], in0=src, scalar=tap, in1=cv[:, c, :],
                                                                 op0=ALU.mult, op1=ALU.add)
                        ins.then_inc(s_chain, 1)
                        chain[0] += 1
                if chunks:
                    dve.wait_ge(s_chain, chain[0])
                    dve.sem_inc(s_cv, len(chunks))
                if j == 4:
                    dve.wait_ge(s_rms, 4 + 3 * w)
                    link(nc.vector.reciprocal(rstd[:, 0:P], rstd[:, 0:P]))
                    nc.vector.tensor_tensor(cv[:, :, :], cv[:, :, :], rstd[:, 0:P].unsqueeze(1).to_broadcast([P, C, P]),
                                            ALU.mult).then_inc(s_xn, 1)
                if j == 5:
                    for b in range(2):
                        dve.wait_ge(s_bank[b], 1 + turn("pw2%d" % w, C) // 2)
                    nc.vector.tensor_tensor(hT[:, :, o0:o0 + P], hT[:, :, o0:o0 + P], sqb[:, :, 0:P], ALU.add
                                            ).then_inc(s_res, 1)

            def body(n, layer, before, after):
                hold(dve, "dve", s_yr, n + 1)
                if not isinstance(n, int) or n:
                    hold(dve, "dve", s_gel, n)
                for k in range(TOPK):
                    hold(dve, "dve", s_u[k % NU], n * (16 * TOPK // NU) + 16 * (k // NU + 1))
                    row = rowsU[:, k % NU, :]
                    nc.vector.tensor_tensor_reduce(out=row, in0=row, in1=yrep, scale=1.0, scalar=0.0, op0=ALU.mult,
                                                   op1=ALU.add, accum_out=dots[:, k:k + 1]).then_inc(s_dot, 1)
                    if k == TOPK // 2 - 1:
                        mid(n)
                hold(dve, "dve", s_exp, n + 1)
                nc.vector.reciprocal(grec[:, :], gsum[:, :])
                hold(dve, "dve", s_gel, n + 1)
                dve.drain()
                nc.vector.scalar_tensor_tensor(out=coef[:, :], in0=gel[:, :], scalar=grec[:, :], in1=gexp[:, :],
                                               op0=ALU.mult, op1=ALU.mult)
                hold(dve, "dve", s_vm, 1 + n * TOPK)
                dve.drain()
                nc.vector.tensor_tensor(mix[:, :, :], coef[:, :].unsqueeze(2).to_broadcast([P, TOPK, GT]),
                                        sel[:, :].unsqueeze(1).to_broadcast([P, TOPK, GT]), ALU.mult).then_inc(s_m, 1)
                if after:
                    route(n + 1, layer_of(n + 1) if isinstance(n, int) else layer)
                if before:
                    add_back(n, layer_of(n - 1) if isinstance(n, int) else layer)
                late(n)

            def add_back(n, layer):
                hold(dve, "dve", s_ot, n + 1)
                hv = hT[:, :, bass.ds(token(n - 1, layer), GT)]
                nc.vector.tensor_tensor(hv, hv, pt, ALU.add).then_inc(s_ha, 1)

            norm(2, yT[:, :, :], hT[:, :, :], ("ffn_g", 0), L, s_y)
            dve.wait_ge(s_pdve, 1)
            route(0, 0)
            pipeline(dve, body)
            add_back(N, 1)
            norm(9, yF, hT[:, :, META:L], ("fin_g", 0), SEQ, s_rdy)


_INS = ['x', 'meta_tokens', 'mix_norm_g', 'ffn_norm_g', 'final_norm_g', 'ab_w_in', 'ab_conv_w', 'ab_w_out', 'cf_w_pw1',
        'cf_b_pw1', 'cf_conv_w', 'cf_conv_b', 'cf_ln_g', 'cf_ln_b', 'cf_w_pw2', 'cf_b_pw2', 'peer_w_q',
        'peer_sub_keys', 'peer_u', 'peer_v']


def kernel(**inputs):
    import numpy as _np
    import concourse.bacc as _bacc
    from concourse import mybir as _mybir
    from concourse.bass_utils import run_bass_kernel_spmd as _run

    nc = _bacc.Bacc("TRN2", target_bir_lowering=False, num_devices=1)
    arrays, args = {}, []
    for name in _INS:
        a = _np.ascontiguousarray(inputs[name])
        arrays[f"in_{name}_dram"] = a
        args.append(nc.dram_tensor(f"in_{name}_dram", a.shape, _mybir.dt.from_np(a.dtype), kind="ExternalInput").ap())
    shape = tuple(inputs["x"].shape)
    args.append(nc.dram_tensor("out_0_dram", shape, _mybir.dt.float32, kind="ExternalOutput").ap())
    hybrid_trunk(nc, *args)
    r = _run(nc, [arrays], core_ids=[0])
    return r.results[0]["out_0_dram"]
```

```python
import concourse.bass as bass
from concourse import mybir
from contextlib import ExitStack


def hybrid_trunk(nc, x, meta_tokens, mix_norm_g, ffn_norm_g, final_norm_g, ab_w_in, ab_conv_w, ab_w_out,
                 cf_w_pw1, cf_b_pw1, cf_conv_w, cf_conv_b, cf_ln_g, cf_ln_b, cf_w_pw2, cf_b_pw2,
                 peer_w_q, peer_sub_keys, peer_u, peer_v, out):
    f32, u32 = mybir.dt.float32, mybir.dt.uint32
    ALU, ACT = mybir.AluOpType, mybir.ActivationFunctionType
    AX = mybir.AxisListType.X

    P = 128
    D = x.shape[2]
    C = D // P
    META = meta_tokens.shape[0]
    SEQ = x.shape[1]
    L = META + SEQ
    TILES = SEQ // P
    AH = 8
    AW = D // 2
    DH = AW // AH
    AC = AW // P
    KC = ab_conv_w.shape[1]
    CK = cf_conv_w.shape[1]
    H = 8
    NK = peer_sub_keys.shape[2]
    NE = peer_u.shape[1]
    TOPK = 16
    GT = P // H
    EPS = 1e-6
    LOW = -3.0e38
    NB = 4
    NU = 8

    KT = [(0, P), (P, P), (2 * P, L - 2 * P)]
    KW = [L - k0 for k0, _ in KT]
    KO = [0, KW[0], KW[0] + KW[1]]
    ZW = sum(KW)

    ctx = ExitStack()
    with ctx:
        def sb(name, shape, dt=f32):
            return ctx.enter_context(nc.sbuf_tensor(name, shape, dt))

        def sem(name):
            return ctx.enter_context(nc.semaphore(name))

        big = sb("big", [P, NU + TOPK, D])
        rowsU = big[:, 0:NU, :]
        rowsV = big[:, NU:NU + TOPK, :]
        flat = big[:, :, :].rearrange("p a b -> p (a b)")
        room = [0]

        def carve(*shape):
            n = 1
            for s in shape:
                n *= s
            a = flat[:, room[0]:room[0] + n]
            room[0] += n
            assert room[0] <= (NU + TOPK) * D
            if len(shape) == 1:
                return a
            if len(shape) == 2:
                return a.rearrange("p (a b) -> p a b", b=shape[1])
            return a.rearrange("p (a b c) -> p a b c", b=shape[1], c=shape[2])

        wring = sb("wring", [P, NB, C, P])
        hT = sb("hT", [P, C, L])
        yT = sb("yT", [P, C, L])
        ident = sb("ident", [P, P])
        ones = sb("ones", [P, P])
        tri = sb("tri", [P, P])
        sel = sb("sel", [P, GT])
        iota16 = sb("iota16", [P, TOPK])
        epsc = sb("epsc", [P, 1])
        keysT = sb("keysT", [P, 4, NK])
        convT = sb("convT", [P, C, CK])
        NPAR = 2 * C + 2 * C + KC * AC + 2 * C + 5 * C - C
        params = sb("params", [P, NPAR])
        rstd = sb("rstd", [P, L])
        yg = sb("yg", [P, C, H, GT])
        qg = sb("qg", [P, 2, H, GT])
        val = sb("val", [P, 2, TOPK])
        idx = sb("idx", [P, 2, TOPK], u32)
        idxf = sb("idxf", [P, 2, TOPK])
        rest = sb("rest", [P, 2, NK])
        cand = sb("cand", [P, TOPK, TOPK])
        cand2 = sb("cand2", [P, TOPK, TOPK])
        topv = sb("topv", [P, TOPK])
        topp = sb("topp", [P, TOPK], u32)
        posu = sb("posu", [P, 2, TOPK], u32)
        posf = sb("posf", [P, 2, TOPK])
        hot = sb("hot", [P, 2, TOPK, TOPK])
        picked = sb("picked", [P, 2, TOPK])
        expU = sb("expU", [P, TOPK], u32)
        expV = sb("expV", [P, TOPK], u32)
        negm = sb("negm", [P, 1])
        gexp = sb("gexp", [P, TOPK])
        gsum = sb("gsum", [P, 1])
        grec = sb("grec", [P, 1])
        dots = sb("dots", [P, TOPK])
        gel = sb("gel", [P, TOPK])
        coef = sb("coef", [P, TOPK])
        mix = sb("mix", [P, TOPK, GT])
        osb = sb("osb", [GT, D])
        qT = sb("qT", [P, H, 2, L])
        hg = sb("hg", [P, C, GT])
        sqo = sb("sqo", [GT, D])
        ssq = sb("ssq", [GT, 1])
        rsq = sb("rsq", [GT, 1])
        gfin = sb("gfin", [GT, D])
        rowsO = sb("rowsO", [GT, D])

        BLOCKS = [(0, L - P, META), (L - P, P, L - P)]
        BW = L - P
        PECONV = (5, 6, 7)
        sqb = sb("sqb", [P, C, BW])
        gz = sb("gz", [P, C, L + CK - 1])
        ga = sb("ga", [P, C // 2, BW])
        sg = sb("sg", [P, C // 2, BW])
        cv = sb("cv", [P, C, P])
        mu = sb("mu", [P, P])

        xin = carve(TILES, D)
        min_ = carve(D)
        kin = carve(4, P)
        cin = carve(D)
        pin = carve(P)
        room[0] = 0
        sq = carve(C, L)
        room[0] = 0
        vtok = carve(3, AW)
        room[0] = C * L
        mixT = carve(C, L)
        cx = carve(AC, L + KC - 1)
        ct = carve(AC, L)
        assert room[0] <= NU * D
        proj = carve(24, L)
        Z = carve(AH, ZW)
        A = carve(AH, ZW)
        S = carve(AH, ZW)
        WQ = 4
        wq0 = rowsV.rearrange("p (i k) d -> p i (k d)", i=WQ).rearrange("p i (c n) -> p i c n", c=C)

        ps = ctx.enter_context(nc.psum_tensor("ps", [P, 8, 512], f32))
        yrep = ps[:, 2:4, :].rearrange("p a b -> p (a b)")
        psc = ps[:, 4, 0:2 * NK]
        po = ps[:, 5:7, :]
        pt = ps[:, 7, 0:C * GT].rearrange("p (c t) -> p c t", t=GT)

        prow = {}
        loads = []
        n = 0
        for name, ap in (("mix_g", mix_norm_g.rearrange("l (c p) -> (l c) p", p=P)),
                         ("ffn_g", ffn_norm_g.rearrange("l (c p) -> (l c) p", p=P)),
                         ("ab_w", ab_conv_w[0].rearrange("k (c p) -> (k c) p", p=P)),
                         ("pw1_b", cf_b_pw1.rearrange("l (c p) -> (l c) p", p=P)),
                         ("cv_b", cf_conv_b.rearrange("l (c p) -> (l c) p", p=P)),
                         ("ln_g", cf_ln_g.rearrange("l (c p) -> (l c) p", p=P)),
                         ("ln_b", cf_ln_b.rearrange("l (c p) -> (l c) p", p=P)),
                         ("pw2_b", cf_b_pw2.rearrange("l (c p) -> (l c) p", p=P))):
            prow[name] = n
            loads.append((n, ap))
            n += ap.shape[0]
        assert n == NPAR <= P

        def par(name, i):
            return params[:, prow[name] + i:prow[name] + i + 1]

        keys_dram = peer_sub_keys.rearrange("l s n c -> n (l s) c")
        u_rows = peer_u.rearrange("l e d -> (l e) d")
        v_rows = peer_v.rearrange("l e d -> (l e) d")

        s_par = sem("s_par")
        s_x = sem("s_x")
        s_keys = sem("s_keys")
        s_cw = sem("s_cw")
        s_w = [sem(f"s_w{b}") for b in range(NB)]
        s_const = sem("s_const")
        s_pdve = sem("s_pdve")
        s_tp = sem("s_tp")
        s_tpe = sem("s_tpe")
        s_sq = sem("s_sq")
        s_ss = sem("s_ss")
        s_rms = sem("s_rms")
        s_y = sem("s_y")
        s_proj = sem("s_proj")
        s_bank = [sem(f"s_bank{b}") for b in range(2)]
        s_vt = sem("s_vt")
        s_vte = sem("s_vte")
        s_z = sem("s_z")
        s_ze = sem("s_ze")
        s_zz = sem("s_zz")
        s_abs = sem("s_abs")
        s_e0 = sem("s_e0")
        s_ln = sem("s_ln")
        s_spl = sem("s_spl")
        s_spm = sem("s_spm")
        s_suf = sem("s_suf")
        s_lw = sem("s_lw")
        s_ew = sem("s_ew")
        s_wm = sem("s_wm")
        s_av = sem("s_av")
        s_ave = sem("s_ave")
        s_b = sem("s_b")
        s_pad = sem("s_pad")
        s_res = sem("s_res")
        s_gz = sem("s_gz")
        s_cv = sem("s_cv")
        s_dg = sem("s_dg")
        s_dgu = sem("s_dgu")
        s_mu = sem("s_mu")
        s_xc = sem("s_xc")
        s_xn = sem("s_xn")
        s_sz = sem("s_sz")
        s_chain = sem("s_chain")
        s_qg = sem("s_qg")
        s_yg = sem("s_yg")
        s_sc = sem("s_sc")
        s_yr = sem("s_yr")
        s_top = sem("s_top")
        s_exp = sem("s_exp")
        s_idx = sem("s_idx")
        s_idv = sem("s_idv")
        s_u = [sem(f"s_u{k}") for k in range(TOPK)]
        s_v = [sem(f"s_v{k}") for k in range(TOPK)]
        s_dot = sem("s_dot")
        s_gel = sem("s_gel")
        s_m = sem("s_m")
        s_vm = sem("s_vm")
        s_oe = sem("s_oe")
        s_ot = sem("s_ot")
        s_ha = sem("s_ha")
        s_wq = [sem(f"s_wq{i}") for i in range(4)]
        s_hg = sem("s_hg")
        s_ssq = sem("s_ssq")
        s_rsq = sem("s_rsq")
        s_fin = sem("s_fin")
        s_gf = sem("s_gf")
        s_out = sem("s_out")
        s_turn = {e: sem("s_turn_" + e) for e in ("pool", "dve", "act", "pe")}

        def hold(eng, name, s, value):
            eng.wait_ge(s, value)
            if not isinstance(value, int):
                eng.sem_inc(s_turn[name], 1)

        w_in, w_out = ab_w_in[0], ab_w_out[0]
        w_pw1, w_pw2 = cf_w_pw1[0], cf_w_pw2[0]
        w_q = [peer_w_q[i] for i in range(2)]
        SEQW = [("in", w_in, 24), ("out", w_out, 8)]
        for i in range(len(BLOCKS)):
            SEQW += [("pw1%d" % i, w_pw1, 16), ("pw2%d" % i, w_pw2, 8), ("q1%d" % i, w_q[1], 16)]
        first, ring = {}, {}
        at = 0
        for name, _, k in SEQW:
            first[name] = at
            ring[name] = at - (first["q0B"] + 16 - first["q0A"] if "q0A" in first else 0)
            at += k
            if name == "out":
                first["q0A"], first["q0B"] = at, at + 16
                at += 32
        sums_before = {"in": 1, "out": 1, "q0A": 2, "q0B": 2}
        for i in range(len(BLOCKS)):
            sums_before.update({"pw1%d" % i: 3 + 4 * i, "pw2%d" % i: 5 + 4 * i, "q1%d" % i: 6 + 4 * i})

        def turn(name, k):
            return first[name] + k + 2 * sums_before[name]

        G0, G1 = L // GT, SEQ // GT
        N = G0 + G1
        GB = BLOCKS[1][0] // GT
        SIDE = 8
        assert GB + SIDE == G0 and G0 + SIDE < N - 1

        def token(n, layer):
            return n * GT - layer * (G0 - 1) * GT

        def layer_of(n):
            return int(n >= G0)

        def step(n):
            if isinstance(n, int) and GB <= n < GB + 2 * SIDE:
                return (n - GB) // SIDE, (n - GB) % SIDE
            return 0, None

        def pipeline(eng, body):
            body(0, 0, False, True)
            with eng.Fori(1, GB) as n:
                body(n, 0, True, True)
            for n in range(GB, GB + 2 * SIDE):
                body(n, layer_of(n), True, True)
            with eng.Fori(GB + 2 * SIDE, N - 1) as n:
                body(n, 1, True, True)
            body(N - 1, 1, True, False)

        block = ctx.enter_context(nc.Block())

        @block.sync
        def _(sp):
            for i in range(TILES):
                sp.dma_start(xin[:, i, :], x[0, i * P:(i + 1) * P, :]).then_inc(s_x, 16)
            sp.dma_start(min_[0:META, :], meta_tokens).then_inc(s_x, 16)

            def chunk(w, b, col):
                return sp.dma_start(wring[:, b, :, :], w.rearrange("(c p) n -> p c n", p=P)[:, :, col]).then_inc(s_w[b], 16)

            for name, w, k in SEQW:
                if first[name] == 0:
                    for b in range(NB):
                        chunk(w, b, bass.ts(b, P))
                    lo = 1
                else:
                    lo = 0
                with sp.Fori(lo, k // NB) if k // NB - lo > 1 else ExitStack() as r:
                    if k // NB - lo <= 1:
                        r = lo
                    for b in range(NB):
                        sp.wait_ge(s_proj, first[name] + r * NB + b - NB + 1)
                        if name[:3] == "pw1":
                            col = bass.ds(r * (NB // 2 * P) + (b % 2) * D + b // 2 * P, P)
                        else:
                            col = bass.ds(r * (NB * P) + b * P, P)
                        chunk(w, b, col)
                if name == "out":
                    sp.wait_ge(s_av, AH)
                    sp.wait_ge(s_b, AC)
                    for i in range(WQ):
                        n = w_q[0].shape[1] // WQ
                        sp.dma_start(wq0[:, i, :, :], w_q[0].rearrange("(c p) n -> p c n", p=P)[:, :, i * n:(i + 1) * n]
                                     ).then_inc(s_wq[i], 16)
            sp.wait_ge(s_out, 16 * G1)

        @block.gpsimd
        def _(pool):
            nc.gpsimd.memset(ident[:, :], 0.0).then_inc(s_const, 1)
            nc.gpsimd.memset(ones[:, :], 1.0).then_inc(s_const, 1)
            nc.gpsimd.memset(epsc[:, :], EPS).then_inc(s_const, 1)
            nc.gpsimd.iota(iota16[:, :], [[1, TOPK]], base=0, channel_multiplier=0,
                           allow_small_or_imprecise_dtypes=True).then_inc(s_const, 1)
            pool.wait_ge(s_const, 4)
            nc.gpsimd.affine_select(out=ident[:, :], in_=ident[:, :], compare_op=ALU.not_equal, fill=1.0, base=0,
                                    pattern=[[-1, P]], channel_multiplier=1).then_inc(s_const, 1)
            nc.gpsimd.affine_select(out=tri[:, :], in_=ones[:, :], compare_op=ALU.is_ge, fill=0.0, base=0,
                                    pattern=[[-1, P]], channel_multiplier=1).then_inc(s_const, 1)
            nc.gpsimd.memset(gz[:, :, 0:CK - 1], 0.0).then_inc(s_pad, 1)
            pool.wait_ge(s_tpe, 8)
            nc.gpsimd.memset(cx[:, :, 0:KC - 1], 0.0).then_inc(s_pad, 1)
            nc.gpsimd.memset(Z[:, :, KO[2]:ZW], 0.0).then_inc(s_zz, 1)

            def mask(t, half, done):
                for (k0, kn), ko in zip(KT, KO):
                    v = t[0:kn, half * (AH // 2):(half + 1) * (AH // 2), ko:ko + kn]
                    nc.gpsimd.affine_select(out=v, in_=v, compare_op=ALU.is_gt, fill=0.0, base=0,
                                            pattern=[[0, AH // 2], [1, kn]], channel_multiplier=-1).then_inc(done, 1)

            for half in range(2):
                pool.wait_ge(s_spl, half + 1)
                mask(S, half, s_spm)
            for half in range(2):
                pool.wait_ge(s_ew, half + 1)
                mask(A, half, s_wm)

            def gathers(n, layer, before, after):
                hold(pool, "pool", s_idx, n + 1)
                for k in range(TOPK):
                    hold(pool, "pool", s_dot, n * TOPK + k + 1)
                    pool.indirect_dma_start(out=rowsU[:, k % NU, :], out_offset=None, in_=u_rows,
                                            in_offset=bass.IndirectOffsetOnAxis(ap=expU[:, k:k + 1], axis=0)
                                            ).then_inc(s_u[k % NU], 16)
                hold(pool, "pool", s_vm, n * TOPK + 1)
                nc.gpsimd.tensor_copy(expV[:, :], expU[:, :]).then_inc(s_idv, 1)
                hold(pool, "pool", s_idv, n + 2)
                for k in range(TOPK):
                    pool.indirect_dma_start(out=rowsV[:, k, :], out_offset=None, in_=v_rows,
                                            in_offset=bass.IndirectOffsetOnAxis(ap=expV[:, k:k + 1], axis=0)
                                            ).then_inc(s_v[k], 16)

            pool.sem_inc(s_idv, 1)
            pool.wait_ge(s_y, 2)
            with pool.Fori(0, N) as n:
                gathers(n, 0, True, True)

        @block.scalar
        def _(act):
            act.sem_inc(s_bank[0], 1)
            act.sem_inc(s_bank[1], 1)
            act.sem_inc(s_ha, 1)
            act.sem_inc(s_ot, 1)
            act.sem_inc(s_dot, NU)
            for r, ap in loads:
                act.dma_start(pin[r:r + ap.shape[0], :], ap).then_inc(s_par, 16)
            act.dma_start(kin, keys_dram).then_inc(s_keys, 16)
            act.dma_start(cin[0:CK, :], cf_conv_w[0]).then_inc(s_cw, 16)
            act.dma_start(gfin[:, :], final_norm_g.unsqueeze(0).to_broadcast([GT, D])).then_inc(s_gf, 16)
            for i in range(TILES):
                act.wait_ge(s_tp, 1 + 2 * i)
                act.copy(hT[:, 0:4, META + i * P:META + (i + 1) * P],
                         ps[:, 1 + 2 * i, :].rearrange("p (c t) -> p c t", t=P)).then_inc(s_tpe, 1)
            act.wait_ge(s_tp, 5)
            act.copy(hT[:, :, 0:META], ps[:, 5, 0:C * META].rearrange("p (c t) -> p c t", t=META)).then_inc(s_tpe, 1)

            def free_both(s, value):
                act.wait_ge(s, value)
                act.sem_inc(s_bank[0], 1)
                act.sem_inc(s_bank[1], 1)

            def root(m, w):
                act.wait_ge(s_ss, m)
                act.activation(rstd[:, 0:w], ps[:, 0, 0:w], ACT.Sqrt, bias=epsc[:, :], scale=1.0 / D).then_inc(s_rms, 1)
                free_both(s_rms, m)

            def evacuate(name, count, dst):
                n0 = first[name]
                with act.Fori(0, count // NB) as r:
                    for b in range(NB):
                        hold(act, "act", s_proj, n0 + r * NB + b + 1)
                        act.copy(dst(r, b), ps[:, b % 2, 0:L]).then_inc(s_bank[b % 2], 1)

            act.wait_ge(s_tpe, 5)
            act.activation(sq[:, :, :], hT[:, :, :], ACT.Square).then_inc(s_sq, 1)
            act.wait_ge(s_tp, 6)
            act.copy(params[:, :], ps[:, 1, 0:NPAR]).then_inc(s_tpe, 1)
            root(1, L)
            act.wait_ge(s_tp, 7)
            act.copy(keysT[:, :, :], ps[:, 6, :].rearrange("p (s k) -> p s k", k=NK)).then_inc(s_tpe, 1)
            act.wait_ge(s_tp, 8)
            act.copy(convT[:, :, :], ps[:, 7, 0:C * CK].rearrange("p (c k) -> p c k", k=CK)).then_inc(s_tpe, 1)
            act.wait_ge(s_tpe, 8)
            evacuate("in", 12, lambda r, b: proj[:, bass.ds(r * NB + b, 1), :].rearrange("p a t -> p (a t)"))
            act.wait_ge(s_zz, 1)
            for h in range(AH):
                act.wait_ge(s_z, h + 1)
                b = 2 + h % 6
                act.activation(Z[:, h, 0:KO[2]], ps[:, b, 0:KO[2]], ACT.Copy, scale=DH ** -0.5).then_inc(s_ze, 1)
                act.activation(Z[0:KT[2][1], h, KO[2]:ZW], ps[0:KT[2][1], b, KO[2]:ZW], ACT.Copy,
                               scale=DH ** -0.5).then_inc(s_ze, 1)
            HH = AH // 2
            for half in range(2):
                a = A[:, half * HH:(half + 1) * HH, :]
                act.wait_ge(s_ze, (half + 1) * AH)
                act.activation(a, Z[:, half * HH:(half + 1) * HH, :], ACT.Abs).then_inc(s_abs, 1)
                act.wait_ge(s_abs, half + 1)
                act.activation(a, a, ACT.Exp, scale=-1.0).then_inc(s_e0, 1)
                act.wait_ge(s_e0, half + 1)
                act.activation(a, a, ACT.Ln, bias=1.0).then_inc(s_ln, 1)
            for half in range(2):
                act.wait_ge(s_lw, (half + 1) * AH)
                act.activation(A[:, half * HH:(half + 1) * HH, :], Z[:, half * HH:(half + 1) * HH, :],
                               ACT.Exp).then_inc(s_ew, 1)
            for c in range(AC):
                act.wait_ge(s_av, 2 * c + 2)
                act.copy(mixT[:, c, :], ps[:, 2 + c, 0:L]).then_inc(s_ave, 1)

            act.wait_ge(s_res, C)
            act.activation(sq[:, :, :], hT[:, :, :], ACT.Square).then_inc(s_sq, 1)
            root(2, L)
            def queries0(half, lo, hi):
                c0, wi, _ = BLOCKS["AB".index(half)]
                for k in range(lo, hi):
                    act.wait_ge(s_proj, first["q0" + half] + k + 1)
                    act.copy(qT[:, k // 2, k % 2, c0:c0 + wi], ps[:, k % 2, 0:wi]).then_inc(s_bank[k % 2], 1)

            def prepare(n, layer):
                if isinstance(n, int) and n in (0, G0):
                    q = ("q0A", 16) if n == 0 else ("q10", 16)
                    act.wait_ge(s_bank[0], 1 + turn(*q) // 2)
                    act.wait_ge(s_bank[1], 1 + turn(*q) // 2)
                if isinstance(n, int) and n == G0 + SIDE:
                    act.wait_ge(s_bank[0], 1 + turn("q11", 16) // 2)
                    act.wait_ge(s_bank[1], 1 + turn("q11", 16) // 2)
                if isinstance(n, int) and n == 1:
                    act.wait_ge(s_bank[0], 1 + turn("q0B", 16) // 2)
                    act.wait_ge(s_bank[1], 1 + turn("q0B", 16) // 2)
                if not (isinstance(n, int) and n == 0):
                    hold(act, "act", s_sc, n)
                act.copy(qg[:, :, :, :], qT[:, :, :, bass.ds(token(n, layer), GT)].rearrange("p h s t -> p s h t")
                         ).then_inc(s_qg, 1)
                if not (isinstance(n, int) and n == 0):
                    hold(act, "act", s_yr, n)
                act.copy(yg[:, :, :, :], yT[:, :, bass.ds(token(n, layer), GT)].unsqueeze(2)
                         .to_broadcast([P, C, H, GT])).then_inc(s_yg, 1)

            def exps(n):
                hold(act, "act", s_top, n + 1)
                act.activation(gexp[:, :], topv[:, :], ACT.Exp, bias=negm[:, :], accum_out=gsum[:, :]
                               ).then_inc(s_exp, 1)

            def early(n):
                w, j = step(n)
                if j == 1:
                    root(3 + 3 * w, BLOCKS[w][1])
                if j == 6:
                    root(5 + 3 * w, P)

            def beside(n):
                w, j = step(n)
                c0, wi, o0 = BLOCKS[w]
                if j in (1, 2):
                    if j == 2 or w:
                        act.wait_ge(s_gz, 2 * w + j - 1)
                    for c in range(C // 2):
                        act.wait_ge(s_proj, first["pw1%d" % w] + (j - 1) * C + 2 * c + 1)
                        act.activation(ga[:, c, 0:wi], ps[:, 0, 0:wi], ACT.Identity,
                                       bias=par("pw1_b", (j - 1) * (C // 2) + c)).then_inc(s_bank[0], 1)
                        act.wait_ge(s_proj, first["pw1%d" % w] + (j - 1) * C + 2 * c + 2)
                        act.activation(sg[:, c, 0:wi], ps[:, 1, 0:wi], ACT.Sigmoid,
                                       bias=par("pw1_b", C + (j - 1) * (C // 2) + c)).then_inc(s_bank[1], 1)
                if j == 3:
                    for i, c in enumerate(PECONV):
                        for k in range(CK):
                            m = (w * len(PECONV) + i) * CK + k
                            if m >= C:
                                act.wait_ge(s_dgu, m - C + 1)
                            act.activation(sqb[:, m % C, 0:P], ident[:, :], ACT.Identity, scale=convT[:, c, k:k + 1]
                                           ).then_inc(s_dg, 1)
                    act.wait_ge(s_dgu, (w + 1) * len(PECONV) * CK)
                    for i, c in enumerate(PECONV):
                        act.activation(cv[:, c, :], ps[:, i % 2, i // 2 * P:(i // 2 + 1) * P], ACT.Identity, bias=par("cv_b", c)).then_inc(s_cv, 1)
                if j == 4:
                    act.wait_ge(s_xc, w + 1)
                    act.activation(sqb[:, :, 0:P], cv[:, :, :], ACT.Square).then_inc(s_sq, 1)
                    root(4 + 3 * w, P)
                if j == 5:
                    for c in range(C):
                        act.wait_ge(s_proj, first["pw2%d" % w] + c + 1)
                        act.activation(sqb[:, c, 0:P], ps[:, c % 2, 0:P], ACT.Identity, bias=par("pw2_b", c)
                                       ).then_inc(s_bank[c % 2], 1)
                if j in (6, 7):
                    for k in range(C):
                        kk = (j - 6) * C + k
                        act.wait_ge(s_proj, first["q1%d" % w] + kk + 1)
                        act.copy(qT[:, kk // 2, kk % 2, o0:o0 + P], ps[:, kk % 2, 0:P]).then_inc(s_bank[kk % 2], 1)

            def late(n):
                w, j = step(n)
                c0, wi, o0 = BLOCKS[w]
                if j == 0:
                    act.wait_ge(s_ha, 1 + n)
                    act.activation(sqb[:, :, 0:wi], hT[:, :, c0:c0 + wi], ACT.Square).then_inc(s_sq, 1)
                if j == 4:
                    act.wait_ge(s_xn, w + 1)
                    for c in range(C):
                        act.activation(cv[:, c, :], cv[:, c, :], ACT.Silu, bias=par("ln_b", c), scale=par("ln_g", c)
                                       ).then_inc(s_sz, 1)
                if j == 5:
                    act.wait_ge(s_res, C + 1 + w)
                    act.activation(sqb[:, :, 0:P], hT[:, :, o0:o0 + P], ACT.Square).then_inc(s_sq, 1)

            def evacuate_output(n, layer):
                hold(act, "act", s_vm, 1 + n * TOPK)
                if layer == 0 or (isinstance(n, int) and n == G0 + 1):
                    hold(act, "act", s_ot, n)
                else:
                    hold(act, "act", s_fin, n - G0 - 1)
                act.copy(osb[:, :], po[0:GT, :, :].rearrange("p a b -> p (a b)")).then_inc(s_oe, 1)

            def residual_of(n):
                act.copy(hg[:, :, :], hT[:, :, bass.ds(token(n, 1), GT)]).then_inc(s_hg, 1)

            def root_of_output(n):
                hold(act, "act", s_oe, n)
                act.activation(sqo[:, :], osb[:, :], ACT.Square, accum_out=ssq[:, :]).then_inc(s_ssq, 1)
                hold(act, "act", s_ssq, n - G0)
                act.activation(rsq[:, :], ssq[:, :], ACT.Sqrt, bias=epsc[0:GT, :], scale=1.0 / D).then_inc(s_rsq, 1)

            def store(n):
                hold(act, "act", s_fin, n - 1 - G0)
                act.dma_start(out[0, bass.ds(token(n - 2, 1) - META, GT), :], rowsO[:, :]).then_inc(s_out, 16)

            def body(n, layer, before, after):
                lb = layer_of(n - 1) if isinstance(n, int) else layer
                nl = layer_of(n + 1) if isinstance(n, int) else layer
                last_step = step(n)[1] == SIDE - 1
                if after and not last_step:
                    prepare(n + 1, nl)
                if before:
                    evacuate_output(n, lb)
                if layer:
                    residual_of(n)
                early(n)
                beside(n)
                if after and last_step:
                    prepare(n + 1, nl)
                hold(act, "act", s_dot, NU + (n + 1) * TOPK)
                act.activation(gel[:, :], dots[:, :], ACT.Gelu).then_inc(s_gel, 1)
                if before and lb:
                    root_of_output(n)
                    if not isinstance(n, int) or n >= G0 + 2:
                        store(n)
                if after:
                    exps(n + 1)
                late(n)

            queries0("A", 0, 16)
            prepare(0, 0)
            queries0("B", 0, 4)
            exps(0)
            queries0("B", 4, 16)
            act.sem_inc(s_vm, 1)
            pipeline(act, body)
            evacuate_output(N, 1)
            root_of_output(N)
            store(N)
            act.wait_ge(s_fin, G1)
            act.dma_start(out[0, SEQ - GT:SEQ, :], rowsO[:, :]).then_inc(s_out, 16)

        @block.tensor
        def _(pe):
            pe.wait_ge(s_const, 6)
            pe.wait_ge(s_x, 16 * (TILES + 1))
            for i in range(TILES):
                for q in range(2):
                    for c in range(4):
                        last = pe.transpose(ps[:, 1 + 2 * i + q, c * P:(c + 1) * P],
                                            xin[:, i, (4 * q + c) * P:(4 * q + c + 1) * P], ident[:, :])
                    last.then_inc(s_tp, 1)
            for c in range(C):
                last = pe.transpose(ps[:, 5, c * META:(c + 1) * META], min_[0:META, c * P:(c + 1) * P],
                                    ident[0:META, 0:META])
            last.then_inc(s_tp, 1)
            pe.wait_ge(s_par, 16 * len(loads))
            pe.wait_ge(s_tpe, 5)
            pe.transpose(ps[:, 1, 0:NPAR], pin[0:NPAR, :], ident[0:NPAR, 0:NPAR]).then_inc(s_tp, 1)

            def sums(src, w, s, ready, name):
                pe.wait_ge(*ready)
                t = turn(name, 0) // 2 - (2 if s is s_mu else 1)
                pe.wait_ge(s_bank[0], t + 1)
                for c in range(C):
                    last = pe.matmul(ps[:, 0, 0:w], ones[:, :], src[:, c, 0:w], start=(c == 0), stop=(c == C - 1))
                last.then_inc(s, 1)

            def chunk(name, k, b, rhs, w, r=0):
                pe.wait_ge(s_w[b], (r + (ring[name] + k) // NB) * 16 + 16)
                pe.wait_ge(s_bank[b % 2], r * (NB // 2) + turn(name, k) // 2 + 1)
                for c in range(C):
                    last = pe.matmul(ps[:, b % 2, 0:w], wring[:, b, c, :], rhs(c), start=(c == 0), stop=(c == C - 1))
                last.then_inc(s_proj, 1)

            def project(name, count, rhs, w):
                with pe.Fori(0, count // NB) as r:
                    for b in range(NB):
                        chunk(name, b, b, rhs, w, r)

            sums(sq, L, s_ss, (s_sq, 1), "in")
            pe.wait_ge(s_keys, 16)
            for k in range(4):
                last = pe.transpose(ps[:, 6, k * NK:(k + 1) * NK], kin[:, k, :], ident[:, :])
            last.then_inc(s_tp, 1)
            pe.wait_ge(s_cw, 16)
            for c in range(C):
                last = pe.transpose(ps[:, 7, c * CK:(c + 1) * CK], cin[0:CK, c * P:(c + 1) * P], ident[0:CK, 0:CK])
            last.then_inc(s_tp, 1)
            pe.wait_ge(s_y, 1)
            project("in", 12, lambda c: yT[:, c, :], L)
            pe.wait_ge(s_tpe, 8)

            def gates(lo):
                for k in range(lo, lo + 4):
                    chunk("in", k, k % NB, lambda c: yT[:, c, :], L)


            pe.wait_ge(s_bank[0], 1 + turn("in", 12) // 2)
            pe.wait_ge(s_bank[1], 1 + turn("in", 12) // 2)
            for t, (k0, kn) in enumerate(KT):
                for c in range(AC):
                    last = pe.transpose(ps[0:kn, 5 + t, c * P:(c + 1) * P], proj[:, 2 * AC + c, k0:k0 + kn], ident[:, :])
                last.then_inc(s_vt, 1)
            for h in range(AH):
                c, q0 = h // 2, DH * (h % 2)
                if h == 3:
                    pe.wait_ge(s_vte, 3)
                if h >= 6:
                    pe.wait_ge(s_ze, 2 * (h - 5))
                for (k0, kn), ko, kw in zip(KT, KO, KW):
                    last = pe.matmul(ps[0:kn, 2 + h % 6, ko:ko + kw], proj[q0:q0 + DH, AC + c, k0:k0 + kn],
                                     proj[q0:q0 + DH, c, k0:L], start=True, stop=True)
                last.then_inc(s_z, 1)
            gates(12)
            gates(16)
            for h in range(AH):
                if h == 0:
                    pe.wait_ge(s_ze, 2 * AH)
                if h == AH // 2:
                    gates(20)
                if h % (AH // 2) == 0:
                    pe.wait_ge(s_spm, 3 * (h // (AH // 2) + 1))
                b = 2 + h % 6
                if h >= 6:
                    pe.wait_ge(s_lw, 2 * (h - 5))
                for i, ((k0, kn), ko, kw) in enumerate(zip(KT, KO, KW)):
                    for j in range(i, 3):
                        (j0, jn), jo, jw = KT[j], KO[j], KW[j]
                        d = j0 - k0
                        last = pe.matmul(ps[0:kn, b, ko + d:ko + kw], (tri if i == j else ones)[0:jn, 0:kn],
                                         S[0:jn, h, jo:jo + jw], start=(j == i), stop=(j == 2))
                last.then_inc(s_suf, 1)
            for h in range(AH):
                if h == 0:
                    pe.wait_ge(s_lw, 2 * AH)
                if h % (AH // 2) == 0:
                    pe.wait_ge(s_wm, 3 * (h // (AH // 2) + 1))
                c, q0 = h // 2, DH * (h % 2)
                for j in range(3):
                    (j0, jn), jo, jw = KT[j], KO[j], KW[j]
                    last = pe.matmul(ps[q0:q0 + DH, 2 + c, j0:L], vtok[0:jn, j, h * DH:(h + 1) * DH],
                                     A[0:jn, h, jo:jo + jw], start=(j == 0), stop=(j == 2))
                last.then_inc(s_av, 1)
            pe.wait_ge(s_ave, AC)
            pe.wait_ge(s_b, AC)
            project("out", 8, lambda c: mixT[:, c, :], L)

            sums(sq, L, s_ss, (s_sq, 2), "q0A")
            pe.wait_ge(s_y, 2)

            def queries0(half):
                c0, wi, _ = BLOCKS["AB".index(half)]
                for k in range(16):
                    if k % (16 // WQ) == 0:
                        pe.wait_ge(s_wq[k // (16 // WQ)], 16)
                    pe.wait_ge(s_bank[k % 2], turn("q0" + half, k) // 2 + 1)
                    for c in range(C):
                        at = k % (16 // WQ) * P
                        last = pe.matmul(ps[:, k % 2, 0:wi], wq0[:, k // (16 // WQ), c, at:at + P],
                                         yT[:, c, c0:c0 + wi], start=(c == 0), stop=(c == C - 1))
                    last.then_inc(s_proj, 1)

            queries0("A")

            def scores(n, layer):
                hold(pe, "pe", s_qg, n + 1)
                if not isinstance(n, int) or n:
                    hold(pe, "pe", s_top, n)
                for s in range(2):
                    last = pe.matmul(psc[:, s * NK:(s + 1) * NK], qg[:, s, :, :].rearrange("p h t -> p (h t)"),
                                     keysT[:, 2 * layer + s, :], start=True, stop=True)
                last.then_inc(s_sc, 1)

            def rows(n):
                hold(pe, "pe", s_yg, n + 1)
                hold(pe, "pe", s_dot, NU + n * TOPK)
                for c in range(C):
                    last = pe.transpose(yrep[:, c * P:(c + 1) * P], yg[:, c, :, :].rearrange("p h t -> p (h t)"),
                                        ident[:, :])
                last.then_inc(s_yr, 1)

            def values(n, layer):
                hold(pe, "pe", s_m, n + 1)
                if layer:
                    hold(pe, "pe", s_hg, n - G0 + 1)
                if not isinstance(n, int) or n:
                    hold(pe, "pe", s_oe, n)
                for k in range(TOPK):
                    hold(pe, "pe", s_v[k], 16 * (n + 1))
                    for q in range(2):
                        last = pe.matmul(po[0:GT, q, :], mix[:, k, :], rowsV[:, k, 512 * q:512 * (q + 1)],
                                         start=(k == 0), stop=(k == TOPK - 1))
                    if k == 0 and layer:
                        for c in range(C):
                            q, at = c // 4, c % 4 * P
                            pe.matmul(po[0:GT, q, at:at + P], hg[:, c, :], ident[:, :], start=False, stop=False)
                    last.then_inc(s_vm, 1)

            def back(n):
                hold(pe, "pe", s_oe, n)
                hold(pe, "pe", s_ha, n)
                for c in range(C):
                    last = pe.transpose(pt[:, c, :], osb[:, c * P:(c + 1) * P], ident[0:GT, 0:GT])
                last.then_inc(s_ot, 1)

            def early(n):
                w, j = step(n)
                c0, wi, o0 = BLOCKS[w]
                if j == 1:
                    sums(sqb, wi, s_ss, (s_sq, 3 + 3 * w), "pw1%d" % w)
                if j == 4:
                    sums(cv, P, s_mu, (s_cv, C * (w + 1)), "pw2%d" % w)
                if j == 6:
                    sums(sqb, P, s_ss, (s_sq, 5 + 3 * w), "q1%d" % w)

            def beside(n):
                w, j = step(n)
                c0, wi, o0 = BLOCKS[w]
                if j in (1, 2):
                    pe.wait_ge(s_y, 3 + 2 * w)
                    for k in range((j - 1) * C, j * C):
                        chunk("pw1%d" % w, k, k % NB, lambda c: yT[:, c, c0:c0 + wi], wi)
                if j == 3:
                    pe.wait_ge(s_pad, 1)
                    pe.wait_ge(s_gz, 2 * w + 2)
                    for i, c in enumerate(PECONV):
                        pe.wait_ge(s_bank[i % 2], turn("pw2%d" % w, 0) // 2 - 1)
                        for k in range(CK):
                            m = (w * len(PECONV) + i) * CK + k
                            pe.wait_ge(s_dg, m + 1)
                            pe.matmul(ps[:, i % 2, i // 2 * P:(i // 2 + 1) * P], sqb[:, m % C, 0:P],
                                      gz[:, c, o0 + k:o0 + k + P], start=(k == 0), stop=(k == CK - 1)).then_inc(s_dgu, 1)
                if j == 4:
                    sums(sqb, P, s_ss, (s_sq, 4 + 3 * w), "pw2%d" % w)
                if j == 5:
                    pe.wait_ge(s_sz, C * (w + 1))
                    for k in range(C):
                        chunk("pw2%d" % w, k, k % NB, lambda c: cv[:, c, :], P)
                if j in (6, 7):
                    pe.wait_ge(s_y, 4 + 2 * w)
                    for k in range((j - 6) * C, (j - 5) * C):
                        chunk("q1%d" % w, k, k % NB, lambda c: yT[:, c, o0:o0 + P], P)

            def body(n, layer, before, after):
                early(n)
                if before and (layer_of(n - 1) if isinstance(n, int) else layer) == 0:
                    back(n)
                last_step = step(n)[1] == SIDE - 1
                nl = layer_of(n + 1) if isinstance(n, int) else layer
                if after and not last_step:
                    scores(n + 1, nl)
                beside(n)
                if after and last_step:
                    scores(n + 1, nl)
                if after:
                    rows(n + 1)
                values(n, layer)

            scores(0, 0)
            rows(0)
            queries0("B")
            pipeline(pe, body)

        @block.vector
        def _(dve):
            chain = [0]

            def link(ins):
                chain[0] += 1
                ins.then_inc(s_chain, 1)
                dve.wait_ge(s_chain, chain[0])

            def norm(m, dst, src, gains, w, done):
                dve.wait_ge(s_rms, m)
                link(nc.vector.reciprocal(rstd[:, 0:w], rstd[:, 0:w]))
                for c in range(C):
                    last = nc.vector.scalar_tensor_tensor(out=dst[:, c, :], in0=src[:, c, :], scalar=par(gains[0], gains[1] + c),
                                                          in1=rstd[:, 0:w], op0=ALU.mult, op1=ALU.mult)
                last.then_inc(done, 1)

            dve.wait_ge(s_const, 6)
            nc.vector.tensor_reduce(out=sel[:, :], in_=ident[:, :].rearrange("p (h t) -> p t h", t=GT), axis=AX,
                                    op=ALU.add).then_inc(s_pdve, 1)
            for i in range(TILES):
                dve.wait_ge(s_tp, 2 + 2 * i)
                nc.vector.tensor_copy(hT[:, 4:8, META + i * P:META + (i + 1) * P],
                                      ps[:, 2 + 2 * i, :].rearrange("p (c t) -> p c t", t=P)).then_inc(s_tpe, 1)
            dve.wait_ge(s_tpe, 6)
            norm(1, yT[:, :, :], hT[:, :, :], ("mix_g", 0), L, s_y)

            for t, (k0, kn) in enumerate(KT):
                dve.wait_ge(s_vt, t + 1)
                nc.vector.tensor_copy(vtok[0:kn, t, :], ps[0:kn, 5 + t, :]).then_inc(s_vte, 1)
            HH = AH // 2
            def gates(lo):
                for k in range(lo, lo + 4):
                    dve.wait_ge(s_proj, first["in"] + k + 1)
                    nc.vector.tensor_copy(proj[:, k, :], ps[:, k % 2, 0:L]).then_inc(s_bank[k % 2], 1)

            def softplus(half):
                sl = slice(half * HH, (half + 1) * HH)
                dve.wait_ge(s_ln, half + 1)
                nc.vector.scalar_tensor_tensor(out=S[:, sl, :].rearrange("p a b -> p (a b)"),
                                               in0=Z[:, sl, :].rearrange("p a b -> p (a b)"), scalar=0.0,
                                               in1=A[:, sl, :].rearrange("p a b -> p (a b)"), op0=ALU.max,
                                               op1=ALU.add).then_inc(s_spl, 1)

            def log_weights(half):
                for h in range(half * HH, (half + 1) * HH):
                    dve.wait_ge(s_suf, h + 1)
                    b = 2 + h % 6
                    nc.vector.tensor_tensor(Z[:, h, 0:KO[2]], Z[:, h, 0:KO[2]], ps[:, b, 0:KO[2]], ALU.subtract
                                            ).then_inc(s_lw, 1)
                    z2 = Z[0:KT[2][1], h, KO[2]:ZW]
                    nc.vector.tensor_tensor(z2, z2, ps[0:KT[2][1], b, KO[2]:ZW], ALU.subtract).then_inc(s_lw, 1)

            gates(12)
            softplus(0)
            gates(16)
            softplus(1)
            log_weights(0)
            gates(20)
            dve.wait_ge(s_pad, 2)
            for b in range(2):
                dve.wait_ge(s_bank[b], 1 + turn("in", 24) // 2)
            link(nc.vector.tensor_tensor(cx[:, :, KC - 1:], proj[:, 4 * AC:5 * AC, :], proj[:, 5 * AC:6 * AC, :], ALU.mult))
            log_weights(1)
            for k in range(KC):
                for c in range(AC):
                    if k == 0:
                        ins = nc.vector.tensor_scalar(ct[:, c, :], cx[:, c, 0:L], par("ab_w", c), None, ALU.mult)
                    else:
                        dve.wait_ge(s_chain, chain[0] - AC + 1)
                        ins = nc.vector.scalar_tensor_tensor(out=ct[:, c, :], in0=cx[:, c, k:k + L],
                                                             scalar=par("ab_w", k * AC + c), in1=ct[:, c, :],
                                                             op0=ALU.mult, op1=ALU.add)
                    ins.then_inc(s_chain, 1)
                    chain[0] += 1
            done = chain[0] - AC + 1
            for c in range(AC):
                dve.wait_ge(s_chain, done + c)
                nc.vector.tensor_tensor(mixT[:, AC + c, :], proj[:, 3 * AC + c, :], ct[:, c, :], ALU.mult).then_inc(s_b, 1)
            for c in range(C):
                dve.wait_ge(s_proj, first["out"] + c + 1)
                nc.vector.tensor_tensor(hT[:, c, :], hT[:, c, :], ps[:, c % 2, 0:L], ALU.add).then_inc(s_res, 1)
                dve.wait_ge(s_res, c + 1)
                dve.sem_inc(s_bank[c % 2], 1)

            def route(n, layer):
                hold(dve, "dve", s_sc, n + 1)
                sc = [psc[:, s * NK:(s + 1) * NK] for s in range(2)]
                for s in range(2):
                    nc.vector.max(val[:, s, 0:8], sc[s])
                dve.drain()
                for s in range(2):
                    nc.vector.max_index(idx[:, s, 0:8], val[:, s, 0:8], sc[s])
                    nc.vector.match_replace(rest[:, s, :], val[:, s, 0:8], sc[s], LOW)
                dve.drain()
                for s in range(2):
                    nc.vector.max(val[:, s, 8:16], rest[:, s, :])
                dve.drain()
                for s in range(2):
                    nc.vector.max_index(idx[:, s, 8:16], val[:, s, 8:16], rest[:, s, :])
                nc.vector.tensor_tensor(cand[:, :, :], val[:, 0, :].unsqueeze(2).to_broadcast([P, TOPK, TOPK]),
                                        val[:, 1, :].unsqueeze(1).to_broadcast([P, TOPK, TOPK]), ALU.add)
                dve.drain()
                c1 = cand[:, :, :].rearrange("p a b -> p (a b)")
                c2 = cand2[:, :, :].rearrange("p a b -> p (a b)")
                nc.vector.max(topv[:, 0:8], c1)
                nc.vector.tensor_scalar(idxf[:, 0, :], idx[:, 0, :], float(NK), None, ALU.mult)
                nc.vector.tensor_scalar(idxf[:, 1, :], idx[:, 1, :], float(layer * NE), None, ALU.add)
                dve.drain()
                nc.vector.max_index(topp[:, 0:8], topv[:, 0:8], c1)
                nc.vector.match_replace(c2, topv[:, 0:8], c1, LOW)
                nc.vector.tensor_scalar(negm[:, :], topv[:, 0:1], -1.0, None, ALU.mult)
                dve.drain()
                nc.vector.max(topv[:, 8:16], c2).then_inc(s_top, 1)
                dve.drain()
                nc.vector.max_index(topp[:, 8:16], topv[:, 8:16], c2)
                dve.drain()
                nc.vector.tensor_scalar(posu[:, 0, :], topp[:, :], 4, None, ALU.logical_shift_right)
                nc.vector.tensor_scalar(posu[:, 1, :], topp[:, :], 15, None, ALU.bitwise_and)
                dve.drain()
                nc.vector.tensor_copy(posf[:, :, :], posu[:, :, :])
                dve.drain()
                for s in range(2):
                    nc.vector.tensor_tensor(hot[:, s, :, :], posf[:, s, :].unsqueeze(2).to_broadcast([P, TOPK, TOPK]),
                                            iota16[:, :].unsqueeze(1).to_broadcast([P, TOPK, TOPK]), ALU.is_equal)
                dve.drain()
                for s in range(2):
                    nc.vector.tensor_tensor(hot[:, s, :, :], hot[:, s, :, :],
                                            idxf[:, s, :].unsqueeze(1).to_broadcast([P, TOPK, TOPK]), ALU.mult)
                dve.drain()
                nc.vector.tensor_reduce(out=picked[:, :, :], in_=hot[:, :, :, :], axis=AX, op=ALU.add)
                dve.drain()
                hold(dve, "dve", s_idv, n + 1)
                nc.vector.tensor_tensor(expU[:, :], picked[:, 0, :], picked[:, 1, :], ALU.add).then_inc(s_idx, 1)

            def mid(n):
                w, j = step(n)
                c0, wi, o0 = BLOCKS[w]
                if j == 1:
                    norm(3 + 3 * w, yT[:, :, c0:c0 + wi], hT[:, :, c0:c0 + wi], ("mix_g", C), wi, s_y)
                if j == 4:
                    dve.wait_ge(s_mu, w + 1)
                    link(nc.vector.tensor_scalar(mu[:, :], ps[:, 0, 0:P], 1.0 / D, None, ALU.mult))
                    dve.sem_inc(s_bank[0], 1)
                    dve.sem_inc(s_bank[1], 1)
                    nc.vector.tensor_tensor(cv[:, :, :], cv[:, :, :], mu[:, :].unsqueeze(1).to_broadcast([P, C, P]),
                                            ALU.subtract).then_inc(s_xc, 1)
                if j == 6:
                    norm(5 + 3 * w, yT[:, :, o0:o0 + P], hT[:, :, o0:o0 + P], ("ffn_g", C), P, s_y)

            def late(n):
                w, j = step(n)
                c0, wi, o0 = BLOCKS[w]
                if j in (1, 2):
                    for b in range(2):
                        dve.wait_ge(s_bank[b], 1 + turn("pw1%d" % w, j * C) // 2)
                    if j == 1:
                        dve.wait_ge(s_pad, 1)
                    half = slice((j - 1) * (C // 2), j * (C // 2))
                    nc.vector.tensor_tensor(gz[:, half, CK - 1 + c0:CK - 1 + c0 + wi], ga[:, :, 0:wi], sg[:, :, 0:wi],
                                            ALU.mult).then_inc(s_gz, 1)
                    dve.wait_ge(s_gz, 2 * w + j)
                chunks = {1: (0, 1), 2: (2, 3), 3: (4,)}.get(j, ())
                for k in range(CK if chunks else 0):
                    for c in chunks:
                        tap, src = convT[:, c, k:k + 1], gz[:, c, o0 + k:o0 + k + P]
                        if k == 0:
                            ins = nc.vector.tensor_scalar(cv[:, c, :], src, tap, par("cv_b", c), ALU.mult, ALU.add)
                        else:
                            dve.wait_ge(s_chain, chain[0] - len(chunks) + 1)
                            ins = nc.vector.scalar_tensor_tensor(out=cv[:, c, :], in0=src, scalar=tap, in1=cv[:, c, :],
                                                                 op0=ALU.mult, op1=ALU.add)
                        ins.then_inc(s_chain, 1)
                        chain[0] += 1
                if chunks:
                    dve.wait_ge(s_chain, chain[0])
                    dve.sem_inc(s_cv, len(chunks))
                if j == 4:
                    dve.wait_ge(s_rms, 4 + 3 * w)
                    link(nc.vector.reciprocal(rstd[:, 0:P], rstd[:, 0:P]))
                    nc.vector.tensor_tensor(cv[:, :, :], cv[:, :, :], rstd[:, 0:P].unsqueeze(1).to_broadcast([P, C, P]),
                                            ALU.mult).then_inc(s_xn, 1)
                if j == 5:
                    for b in range(2):
                        dve.wait_ge(s_bank[b], 1 + turn("pw2%d" % w, C) // 2)
                    nc.vector.tensor_tensor(hT[:, :, o0:o0 + P], hT[:, :, o0:o0 + P], sqb[:, :, 0:P], ALU.add
                                            ).then_inc(s_res, 1)

            def body(n, layer, before, after):
                hold(dve, "dve", s_yr, n + 1)
                if not isinstance(n, int) or n:
                    hold(dve, "dve", s_gel, n)
                for k in range(TOPK):
                    hold(dve, "dve", s_u[k % NU], n * (16 * TOPK // NU) + 16 * (k // NU + 1))
                    row = rowsU[:, k % NU, :]
                    nc.vector.tensor_tensor_reduce(out=row, in0=row, in1=yrep, scale=1.0, scalar=0.0, op0=ALU.mult,
                                                   op1=ALU.add, accum_out=dots[:, k:k + 1]).then_inc(s_dot, 1)
                    if k == TOPK // 2 - 1:
                        mid(n)
                hold(dve, "dve", s_exp, n + 1)
                nc.vector.reciprocal(grec[:, :], gsum[:, :])
                hold(dve, "dve", s_gel, n + 1)
                dve.drain()
                nc.vector.scalar_tensor_tensor(out=coef[:, :], in0=gel[:, :], scalar=grec[:, :], in1=gexp[:, :],
                                               op0=ALU.mult, op1=ALU.mult)
                hold(dve, "dve", s_vm, 1 + n * TOPK)
                dve.drain()
                nc.vector.tensor_tensor(mix[:, :, :], coef[:, :].unsqueeze(2).to_broadcast([P, TOPK, GT]),
                                        sel[:, :].unsqueeze(1).to_broadcast([P, TOPK, GT]), ALU.mult).then_inc(s_m, 1)
                if after:
                    route(n + 1, layer_of(n + 1) if isinstance(n, int) else layer)
                if before:
                    if (layer_of(n - 1) if isinstance(n, int) else layer) == 0:
                        add_back(n, 0)
                    else:
                        finish(n)
                late(n)

            def add_back(n, layer):
                hold(dve, "dve", s_ot, n + 1)
                hv = hT[:, :, bass.ds(token(n - 1, layer), GT)]
                nc.vector.tensor_tensor(hv, hv, pt, ALU.add).then_inc(s_ha, 1)

            def finish(n):
                m = n - 1 - G0
                hold(dve, "dve", s_rsq, m + 1)
                nc.vector.reciprocal(rsq[:, :], rsq[:, :])
                if not isinstance(m, int) or m:
                    hold(dve, "dve", s_out, 16 * m)
                dve.drain()
                nc.vector.scalar_tensor_tensor(out=rowsO[:, :], in0=osb[:, :], scalar=rsq[:, :], in1=gfin[:, :],
                                               op0=ALU.mult, op1=ALU.mult).then_inc(s_fin, 1)

            norm(2, yT[:, :, :], hT[:, :, :], ("ffn_g", 0), L, s_y)
            dve.wait_ge(s_pdve, 1)
            dve.wait_ge(s_gf, 16)
            route(0, 0)
            pipeline(dve, body)
            finish(N)


_INS = ['x', 'meta_tokens', 'mix_norm_g', 'ffn_norm_g', 'final_norm_g', 'ab_w_in', 'ab_conv_w', 'ab_w_out', 'cf_w_pw1',
        'cf_b_pw1', 'cf_conv_w', 'cf_conv_b', 'cf_ln_g', 'cf_ln_b', 'cf_w_pw2', 'cf_b_pw2', 'peer_w_q',
        'peer_sub_keys', 'peer_u', 'peer_v']


def kernel(**inputs):
    import numpy as _np
    import concourse.bacc as _bacc
    from concourse import mybir as _mybir
    from concourse.bass_utils import run_bass_kernel_spmd as _run

    nc = _bacc.Bacc("TRN2", target_bir_lowering=False, num_devices=1)
    arrays, args = {}, []
    for name in _INS:
        a = _np.ascontiguousarray(inputs[name])
        arrays[f"in_{name}_dram"] = a
        args.append(nc.dram_tensor(f"in_{name}_dram", a.shape, _mybir.dt.from_np(a.dtype), kind="ExternalInput").ap())
    shape = tuple(inputs["x"].shape)
    args.append(nc.dram_tensor("out_0_dram", shape, _mybir.dt.float32, kind="ExternalOutput").ap())
    hybrid_trunk(nc, *args)
    r = _run(nc, [arrays], core_ids=[0])
    return r.results[0]["out_0_dram"]
```
